# Optimizing a Trainium2 kernel written in Bass

```python
import jax, jax.numpy as jnp
from jax import lax
import numpy as np

D_MODEL = 1024
BATCH = 1
SEQ = 512
DEPTH = 1
DEC_BATCH = 8
DEC_SEQ = 8
PAST_LEN = 4096
PAGE_SIZE = 128

D_MIX = D_MODEL
D_A = D_MIX // 2
D_B = D_MIX - D_A
GROUP_DIM = 64
N_GROUPS_A = D_A // GROUP_DIM
N_GROUPS_B = D_B // GROUP_DIM
CONV_A = 3
CONV_B = 31
IN_COLS = 3 * D_A + 2 * D_B
N_EXPERT_GROUPS = 4
EXPERTS_PER_GROUP = 8
N_EXPERTS = N_EXPERT_GROUPS * EXPERTS_PER_GROUP
TOP_K_FINE = 2
D_EXPERT = D_MODEL // 4
RMS_EPS = 1e-6
LN_EPS = 1e-5

kernel_name = "hymba_conv_hier_moe_step"

def _rmsnorm(x, g):
    xf = x.astype(jnp.float32)
    y = xf * lax.rsqrt(jnp.mean(xf * xf, axis=-1, keepdims=True) + RMS_EPS)
    return (y * g.astype(jnp.float32)).astype(x.dtype)

def _layernorm(x, g, b):
    xf = x.astype(jnp.float32)
    mu = jnp.mean(xf, axis=-1, keepdims=True)
    var = jnp.mean(jnp.square(xf - mu), axis=-1, keepdims=True)
    y = (xf - mu) * lax.rsqrt(var + LN_EPS)
    return (y * g.astype(jnp.float32) + b.astype(jnp.float32)).astype(x.dtype)

def _causal_dwconv(u_pad, w):
    c = u_pad.shape[-1]
    return lax.conv_general_dilated(
        u_pad, w[:, None, :].astype(u_pad.dtype), window_strides=(1,), padding='VALID',
        dimension_numbers=('NWC', 'WIO', 'NWC'), feature_group_count=c)

def _hier_moe(h, w_coarse, b_coarse, w_fine, b_fine, w_gate, w_up, w_down):
    n, t_len, d = h.shape
    t = h.reshape(n * t_len, d)
    coarse_logits = (t @ w_coarse).astype(jnp.float32) + b_coarse.astype(jnp.float32)
    coarse_prob = jax.nn.softmax(coarse_logits, axis=-1)
    grp = jnp.argmax(coarse_logits, axis=-1)
    p_grp = jnp.take_along_axis(coarse_prob, grp[:, None], axis=-1)
    fine_logits = jnp.einsum('td,gde->tge', t, w_fine).astype(jnp.float32) + b_fine.astype(jnp.float32)
    fine_sel = jnp.take_along_axis(fine_logits, grp[:, None, None], axis=1)[:, 0]
    top_v, top_i = lax.top_k(fine_sel, TOP_K_FINE)
    p_exp = jax.nn.softmax(top_v, axis=-1) * p_grp
    expert_idx = grp[:, None] * EXPERTS_PER_GROUP + top_i
    combine = jnp.sum(jax.nn.one_hot(expert_idx, N_EXPERTS, dtype=jnp.float32) * p_exp[..., None], axis=1)
    out = jnp.zeros((n * t_len, d), jnp.float32)
    for e in range(N_EXPERTS):
        hid = jax.nn.silu(t @ w_gate[e]) * (t @ w_up[e])
        out = out + combine[:, e:e + 1] * (hid @ w_down[e]).astype(jnp.float32)
    return out.astype(h.dtype).reshape(n, t_len, d)

def _layer(x, prev_a, prev_b, g_mix, w_in, conv_a_w, conv_b_w, conv_b_bias, ln_g, ln_b, w_out,
           g_ffn, w_coarse, b_coarse, w_fine, b_fine, w_gate, w_up, w_down):
    h = _rmsnorm(x, g_mix)
    proj = h @ w_in
    b_a = proj[..., :D_A]
    c_a = proj[..., D_A:2 * D_A]
    v_a = proj[..., 2 * D_A:3 * D_A]
    v_b = proj[..., 3 * D_A:3 * D_A + D_B]
    g_b = proj[..., 3 * D_A + D_B:]
    u_pad = jnp.concatenate([prev_a.astype(x.dtype), c_a * v_a], axis=1)
    z_a = b_a * _causal_dwconv(u_pad, conv_a_w)
    new_a = u_pad[:, -(CONV_A - 1):]
    g_pad = jnp.concatenate([prev_b.astype(x.dtype), v_b * jax.nn.sigmoid(g_b)], axis=1)
    z_b = _causal_dwconv(g_pad, conv_b_w) + conv_b_bias
    z_b = jax.nn.silu(_layernorm(z_b, ln_g, ln_b))
    new_b = g_pad[:, -(CONV_B - 1):]
    x = x + jnp.concatenate([z_a, z_b], axis=-1) @ w_out
    x = x + _hier_moe(_rmsnorm(x, g_ffn), w_coarse, b_coarse, w_fine, b_fine, w_gate, w_up, w_down)
    return x, new_a, new_b

def setup_inputs(seed: int = 0) -> dict:
    key = jax.random.key(seed)
    ks = jax.random.split(key, 24)
    f32 = jnp.float32
    nrm = lambda k, shape, s: jax.random.normal(k, shape, f32) * s
    return {
        "x_prompt": nrm(ks[0], (BATCH, SEQ, D_MODEL), 1.0),
        "x_sample": nrm(ks[1], (DEC_BATCH, DEC_SEQ, D_MODEL), 1.0),
        "state_conv_a": nrm(ks[2], (DEPTH, DEC_BATCH, CONV_A - 1, D_A), 1.0),
        "state_conv_b": nrm(ks[3], (DEPTH, DEC_BATCH, CONV_B - 1, D_B), 1.0),
        "g_mix": 1.0 + nrm(ks[4], (DEPTH, D_MODEL), 0.02),
        "w_in": nrm(ks[5], (DEPTH, D_MODEL, IN_COLS), D_MODEL ** -0.5),
        "conv_a_w": nrm(ks[6], (DEPTH, CONV_A, D_A), CONV_A ** -0.5),
        "conv_b_w": nrm(ks[7], (DEPTH, CONV_B, D_B), CONV_B ** -0.5),
        "conv_b_bias": nrm(ks[8], (DEPTH, D_B), 0.02),
        "ln_g": 1.0 + nrm(ks[9], (DEPTH, D_B), 0.02),
        "ln_b": nrm(ks[10], (DEPTH, D_B), 0.02),
        "w_out": nrm(ks[11], (DEPTH, D_MIX, D_MODEL), D_MIX ** -0.5),
        "g_ffn": 1.0 + nrm(ks[12], (DEPTH, D_MODEL), 0.02),
        "w_coarse": nrm(ks[13], (DEPTH, D_MODEL, N_EXPERT_GROUPS), D_MODEL ** -0.5),
        "b_coarse": nrm(ks[14], (DEPTH, N_EXPERT_GROUPS), 0.01),
        "w_fine": nrm(ks[15], (DEPTH, N_EXPERT_GROUPS, D_MODEL, EXPERTS_PER_GROUP), D_MODEL ** -0.5),
        "b_fine": nrm(ks[16], (DEPTH, N_EXPERT_GROUPS, EXPERTS_PER_GROUP), 0.01),
        "w_gate": nrm(ks[17], (DEPTH, N_EXPERTS, D_MODEL, D_EXPERT), D_MODEL ** -0.5),
        "w_up": nrm(ks[18], (DEPTH, N_EXPERTS, D_MODEL, D_EXPERT), D_MODEL ** -0.5),
        "w_down": nrm(ks[19], (DEPTH, N_EXPERTS, D_EXPERT, D_MODEL), D_EXPERT ** -0.5),
        "g_final": 1.0 + nrm(ks[20], (D_MODEL,), 0.02),
    }

def reference(x_prompt, x_sample, state_conv_a, state_conv_b, g_mix, w_in, conv_a_w, conv_b_w,
              conv_b_bias, ln_g, ln_b, w_out, g_ffn, w_coarse, b_coarse, w_fine, b_fine,
              w_gate, w_up, w_down, g_final):
    xp, xs = x_prompt, x_sample
    na_p, nb_p, na_s, nb_s = [], [], [], []
    for l in range(DEPTH):
        params = (g_mix[l], w_in[l], conv_a_w[l], conv_b_w[l], conv_b_bias[l], ln_g[l], ln_b[l],
                  w_out[l], g_ffn[l], w_coarse[l], b_coarse[l], w_fine[l], b_fine[l],
                  w_gate[l], w_up[l], w_down[l])
        zero_a = jnp.zeros((xp.shape[0], CONV_A - 1, D_A), xp.dtype)
        zero_b = jnp.zeros((xp.shape[0], CONV_B - 1, D_B), xp.dtype)
        xp, a_p, b_p = _layer(xp, zero_a, zero_b, *params)
        xs, a_s, b_s = _layer(xs, state_conv_a[l], state_conv_b[l], *params)
        na_p.append(a_p); nb_p.append(b_p); na_s.append(a_s); nb_s.append(b_s)
    y_prompt = _rmsnorm(xp, g_final)
    y_sample = _rmsnorm(xs, g_final)
    new_conv_a_prompt = jnp.stack(na_p, axis=0)
    new_conv_b_prompt = jnp.stack(nb_p, axis=0)
    new_conv_a_sample = jnp.stack(na_s, axis=0)
    new_conv_b_sample = jnp.stack(nb_s, axis=0)
    return (y_prompt, y_sample, new_conv_a_prompt, new_conv_b_prompt, new_conv_a_sample, new_conv_b_sample)


_drawn_inputs = setup_inputs


def setup_inputs(seed=0):
    import zlib

    import numpy as np

    out = dict(_drawn_inputs(seed))
    spreads = {}
    factors = {'conv_b_bias': 3.144,
     'ln_g': 8.981,
     'ln_b': 3.759,
     'b_coarse': 11.549,
     'b_fine': 13.663,
     'g_final': 25.722,
     'g_ffn': 3.09}
    for name, (base, spread) in spreads.items():
        noise = np.random.default_rng([zlib.crc32(name.encode()), seed]).standard_normal(out[name].shape)
        drawn = base * np.exp(spread * noise) if base else spread * noise
        out[name] = __import__('jax').numpy.asarray(drawn.astype(out[name].dtype))
    for name, factor in factors.items():
        out[name] = (out[name] * factor).astype(out[name].dtype)
    return out
```

```python
import concourse.bass as bass
from concourse import mybir
from contextlib import ExitStack

D = 1024
P = 128
KC = D // P
SEQ = 512
NS, SL = 8, 8
NTOK = SEQ + NS * SL
NT = (NTOK + P - 1) // P
TROWS = [min(P, NTOK - t * P) for t in range(NT)]
HALF = NTOK // 2
DA = 512
CC = DA // P
KA, KB = 3, 31
HA, HB = KA - 1, KB - 1
UA = HA + SEQ + NS * (HA + SL)
UB = HB + SEQ + NS * (HB + SL)
SA, SB = HA + SEQ, HB + SEQ
WA, WB = HA + SL, HB + SL
NG, EG = 4, 8
NE = NG * EG
F = 256
T = 64
NSLOT = 4
NBLK = NE + (2 * NTOK - 1) // T
NIDX = NBLK + 1
NTHR = (NTOK - 1) // T
RMS_EPS, LN_EPS = 1e-6, 1e-5


def build_step(nc, a, out):
    fp32, bf16 = mybir.dt.float32, mybir.dt.bfloat16
    i32, u32 = mybir.dt.int32, mybir.dt.uint32
    ALU = mybir.AluOpType
    ACT = mybir.ActivationFunctionType
    AX = mybir.AxisListType
    y_prompt, y_sample, na_p, nb_p, na_s, nb_s = out

    ctx = ExitStack()
    with ctx:
        def sb(name, shape, dt=fp32):
            return ctx.enter_context(nc.sbuf_tensor(name, shape, dt))

        def sem(name):
            return ctx.enter_context(nc.semaphore(name))

        h2_dram = nc.dram_tensor("h2_rows", (NTOK, D), fp32, kind="Internal").ap()
        y_dram = nc.dram_tensor("slot_rows", (NBLK * T, D), fp32, kind="Internal").ap()

        WEXP = 2 * KC * F + (F // P) * D
        RX = sb("region_x", [P, NT * D])
        RH = sb("region_h", [P, NT * D])
        RW = sb("region_w", [P, 5 * KC * DA])
        SLOT0 = sb("slot0", [P, WEXP])
        ub_t = sb("ub", [P, CC * UB])
        ua_t = sb("ua", [P, CC * UA])
        z_t = sb("z", [P, KC * NTOK])

        x_in = RX[:, :].rearrange("p (t d) -> p t d", t=NT)
        hT = RH[:, 0:KC * NTOK].rearrange("p (k n) -> p k n", k=KC)
        zeros = RH[:, KC * NTOK:KC * NTOK + D // 2]
        x1 = RH[:, :].rearrange("p (t d) -> p t d", t=NT)
        SEC = KC * DA
        sec = {n: RW[:, i * SEC:(i + 1) * SEC].rearrange("p (k n) -> p k n", k=KC)
               for i, n in enumerate(["vb", "gb", "c", "va", "b"])}
        w_out_sb = RW[:, 0:2 * SEC].rearrange("p (k n) -> p k n", k=KC)
        slot = [SLOT0[:, :], RW[:, 2 * SEC:2 * SEC + WEXP], RW[:, 2 * SEC + WEXP:2 * SEC + 2 * WEXP],
                RW[:, 0:WEXP]]
        ub = ub_t[:, :].rearrange("p (c n) -> p c n", c=CC)
        ua = ua_t[:, :].rearrange("p (c n) -> p c n", c=CC)
        z = z_t[:, :].rearrange("p (c n) -> p c n", c=KC)
        xn = z_t[:, 0:2 * D].rearrange("p (b d) -> p b d", b=2)
        sqj = z_t[:, 2 * D:3 * D]
        st = [RX[:, i * NTOK:(i + 1) * NTOK] for i in range(5)]
        tA = RX[:, 5 * NTOK:5 * NTOK + UA]
        tB = RX[:, 5 * NTOK + UA:5 * NTOK + 2 * UA]
        rs = RX[:, 5 * NTOK + 2 * UA:6 * NTOK + 2 * UA]
        sq = ub_t[:, 0:CC * NTOK].rearrange("p (c n) -> p c n", c=CC)
        h2 = RX[:, 0:2 * D].rearrange("p (b d) -> p b d", b=2)
        h2T = RX[:, 2 * D:4 * D].rearrange("p (b k n) -> p b k n", b=2, k=KC)
        sq2 = RX[:, 4 * D:5 * D]
        gffn = ub_t[:, D:2 * D]
        gfin = ub_t[:, 0:D]
        xrow = ub_t[0:T, D:2 * D]
        xT = ub_t[:, 2 * D:2 * D + KC * T].rearrange("p (k n) -> p k n", k=KC)
        yblk = ub_t[:, 2 * D + KC * T:2 * D + KC * T + D // 2]
        sg_m = ua_t[:, 0:P]
        hid = ua_t[:, P:2 * P]
        hidT = ua_t[:, 2 * P:3 * P]
        yg = [[(SLOT0 if k == 0 else RW)[:, t * D:(t + 1) * D] for t in range(NT)] for k in range(2)]

        ident = sb("ident", [P, P])
        lnmean = sb("lnmean", [P, P])
        before = sb("before", [P, P], bf16)
        onesb = sb("onesb", [P, P], bf16)
        pst = sb("pst", [P, DA])
        prow = pst[0:KB + KA + 3, :]
        grow = sb("grow", [KC, P])
        par = sb("par", [P, CC * (KB + KA + 3)])
        gmix = sb("gmix", [P, KC])
        sa_rows = sb("sa_rows", [NS * HA, DA])
        sb_rows = sb("sb_rows", [P, 2 * DA])
        st_b = sb_rows
        st_p = pst
        hist_b = sb("hist_b", [P, CC * NS * HB])[:, :].rearrange("p (c n) -> p c n", c=CC)
        hist_a = sb("hist_a", [P, CC * NS * HA])[:, :].rearrange("p (c n) -> p c n", c=CC)
        wr = sb("wr", [P, KC * (NG + NE)])
        rbias = sb("rbias", [P, NG + NE])
        small = sb("small", [P, 64])
        lg = sb("lg", [P, NT * (NG + NE)])
        rt = sb("rt", [P, 1100])
        rti = sb("rti", [P, 160], i32)
        rtu = sb("rtu", [P, 160], u32)
        maskb = sb("maskb", [P, NT * NE], bf16)
        inv_u = sb("inv_u", [T, NIDX], u32)
        idxcol = sb("idxcol", [T, 1], u32)
        bound = sb("bound", [1, NE + 1], i32)

        eps_rms, eps_ln = small[:, 60:61], small[:, 61:62]
        carry = sb("carry", [P, 4])[:, :]
        NCON = 2 + 2 * CC + 2 + 5 + 2 + 4
        NP = KB + KA + 3
        parv = par[:, :].rearrange("p (c n) -> p c n", c=CC)

        def wB(c, j):
            return parv[:, c, j:j + 1]

        def wA(c, j):
            return parv[:, c, KB + j:KB + j + 1]

        ps = [ctx.enter_context(nc.psum_tensor(f"bank{i}", [P, 512], fp32)) for i in range(8)]
        pair_t = [None] * 3

        s_x = [sem(f"s_xin{t}") for t in range(NT)]
        s_par = sem("s_par")
        s_rp = sem("s_rp")
        s_w = {n: sem(f"s_w_{n}") for n in ["vb", "gb", "c", "va", "b"]}
        s_wout = sem("s_wout")
        s_xr = sem("s_xr")
        s_gf = sem("s_gf")
        s_gfin = sem("s_gfin")
        s_const = sem("s_const")
        s_const0 = sem("s_const0")
        s_sq1 = sem("s_sq1")
        s_rms1, s_rms2, s_rms3, s_lnsd = sem("s_rms1"), sem("s_rms2"), sem("s_rms3"), sem("s_lnsd")
        s_xn = sem("s_xn")
        s_xT = sem("s_xT")
        s_hT = sem("s_hT")
        s_pT = sem("s_pT")
        s_pe_par = sem("s_pe_par")
        s_chunk = sem("s_chunk")
        s_evac = sem("s_evac")
        s_ub = sem("s_ub")
        s_uap = sem("s_uap")
        s_ua = sem("s_ua")
        s_za = sem("s_za")
        s_pa = sem("s_pa")
        s_conv = sem("s_conv")
        s_cb = sem("s_cb")
        s_mu = sem("s_mu")
        s_dev = sem("s_dev")
        s_sqb = sem("s_sqb")
        s_var = sem("s_var")
        s_zn = sem("s_zn")
        s_zb = sem("s_zb")
        s_hist = sem("s_hist")
        s_histc = sem("s_histc")
        s_packb = sem("s_packb")
        s_packa = sem("s_packa")
        s_hout = sem("s_hout")
        s_o = sem("s_o")
        s_x1 = sem("s_x1")
        s_sq2 = sem("s_sq2")
        s_h2 = sem("s_h2")
        s_h2d = [sem(f"s_h2d{i}") for i in range(2)]
        s_h2t = sem("s_h2t")
        s_h2T = sem("s_h2T")
        s_lg = sem("s_lg")
        s_lgc = sem("s_lgc")
        s_dve = sem("s_dve")
        s_ex = sem("s_ex")
        s_mask = sem("s_mask")
        s_rank = sem("s_rank")
        s_ab = sem("s_ab")
        s_inv = sem("s_inv")
        s_tab = sem("s_tab")
        s_route = sem("s_route")
        s_idx = sem("s_idx")
        s_gath = sem("s_gath")
        s_xt_ps = sem("s_xt_ps")
        s_xt = sem("s_xt")
        s_gu = sem("s_gu")
        s_silu = sem("s_silu")
        s_hid = sem("s_hid")
        s_hT_ps = sem("s_hT_ps")
        s_hidT = sem("s_hidT")
        s_down = sem("s_down")
        s_yc = sem("s_yc")
        s_yst = sem("s_yst")
        s_wexp = [sem(f"s_wexp{i}") for i in range(NSLOT)]
        s_yg = [sem(f"s_yg{t}") for t in range(NT)]
        s_sq3 = sem("s_sq3")
        s_fin = sem("s_fin")
        s_out = sem("s_out")

        def col(at, n):
            return rt[:, at:at + n]

        iota32 = col(0, NE)
        iotaq = col(32, NIDX)
        iotar = col(96, T)
        iota4 = col(160, NG)
        thr = col(168, NTHR)
        tokf = col(180, NT)
        mx4 = col(190, NT)
        pgr = col(200, NT)
        ngm = col(210, NT)
        w12 = col(220, 2 * NT)
        slf = col(232, 2 * NT)
        cnt = col(244, NE)
        nb = col(276, NE)
        pfx = [col(308, NE), col(340, NE)]
        sbase = col(372, NE)
        m8 = col(404, 8)
        v8 = col(412, 8 * NT)
        grpf = col(452, NT)
        eid = col(458, 2 * NT)
        qf = col(470, 2 * NT)
        rf = col(482, 2 * NT)
        e4 = col(494, NG * NT)
        fsel = col(516, EG * NT)
        oh4 = col(556, NG)
        m12 = col(562, 2 * NE)
        cmp = col(626, NE * NTHR)
        dlt = col(884, NT)
        onesc = col(890, 2)
        p32 = col(892, NE)
        aq = col(924, NIDX)
        br_ = col(976, T)
        ev = col(1042, 2 * NT)

        lgv = lg[:, :].rearrange("p (t n) -> p t n", t=NT)
        wrv = wr[:, :].rearrange("p (k n) -> p k n", k=KC)

        def pairview(i):
            return [ps[2 * i][:, 0:HALF], ps[2 * i + 1][:, 0:HALF]]

        def sample(ap, start, width, lo, n):
            return ap[:, start:start + NS * width].rearrange("p (s w) -> p s w", s=NS)[:, :, lo:lo + n]

        block = ctx.enter_context(nc.Block())

        @block.sync
        def _(sp):
            xp, xs = a["x_prompt"][0], a["x_sample"].rearrange("s l d -> (s l) d")

            def rows_of(t):
                return xp[t * P:(t + 1) * P, :] if t < NT - 1 else xs[:, :]

            for t in range(NT):
                sp.dma_start(x_in[0:TROWS[t], t, :], rows_of(t)).then_inc(s_x[t], 16)
            cols = {"b": 0, "c": 1, "va": 2, "vb": 3, "gb": 4}
            w_in = a["w_in"][0].rearrange("(k p) n -> p k n", p=P)
            for n in ["vb", "gb", "c", "va", "b"]:
                sp.dma_start(sec[n], w_in[:, :, cols[n] * DA:(cols[n] + 1) * DA]).then_inc(s_w[n], 16)

            def load_expert(i, e):
                wg = a["w_gate"][0].rearrange("e (k p) f -> p e k f", p=P)
                wu = a["w_up"][0].rearrange("e (k p) f -> p e k f", p=P)
                wd = a["w_down"][0].rearrange("e (c p) d -> p e c d", p=P)
                half = KC * F
                for src, lo, k in ((wg, 0, KC), (wu, half, KC), (wd, 2 * half, F // P)):
                    n = half if k == KC else (F // P) * D
                    sp.dma_start(slot[i][:, lo:lo + n].rearrange("p (k f) -> p k f", k=k),
                                 src[:, bass.ds(e, 1), :, :].rearrange("p e k f -> p (e k) f"))\
                      .then_inc(s_wexp[i], 16)

            load_expert(0, 0)
            sp.wait_ge(s_chunk, 2 * CC)
            sp.dma_start(w_out_sb, a["w_out"][0].rearrange("(k p) n -> p k n", p=P)).then_inc(s_wout, 16)
            sp.wait_ge(s_chunk, 5 * CC)
            sp.wait_ge(s_yst, 16)
            for t in range(NT):
                sp.dma_start(x1[0:TROWS[t], t, :], rows_of(t)).then_inc(s_xr, 16)
            load_expert(1, 1)
            load_expert(2, 2)
            sp.wait_ge(s_o, NT)
            load_expert(3, 3)
            sp.wait_ge(s_tab, 1)
            with sp.Fori(1, NE // NSLOT) as it:
                for i in range(NSLOT):
                    last = sp.value_load(bound[0:1, bass.ds(it * NSLOT + (i + 1 - NSLOT), 1)],
                                         min_val=1, max_val=NBLK)
                    sp.wait_ge(s_down, last)
                    load_expert(i, it * NSLOT + i)

        @block.scalar
        def _(act):
            r = 0
            for name, n in (("conv_b_w", KB), ("conv_a_w", KA)):
                act.dma_start(prow[r:r + n, :], a[name][0]).then_inc(s_par, 16)
                r += n
            for name in ("conv_b_bias", "ln_g", "ln_b"):
                act.dma_start(prow[r:r + 1, :], a[name]).then_inc(s_par, 16)
                r += 1
            act.dma_start(grow[:, :], a["g_mix"][0].rearrange("(k p) -> k p", p=P)).then_inc(s_par, 16)
            act.dma_start(sa_rows[:, :], a["state_conv_a"][0].rearrange("s j c -> (s j) c")).then_inc(s_par, 16)
            hb = a["state_conv_b"][0].rearrange("s j c -> (s j) c")
            QR = NS * HB // 2
            for i in range(2):
                act.dma_start(sb_rows[0:QR, i * DA:(i + 1) * DA], hb[i * QR:(i + 1) * QR, :]).then_inc(s_par, 16)
            act.dma_start(wrv[:, :, 0:NG], a["w_coarse"][0].rearrange("(k p) g -> p k g", p=P)).then_inc(s_rp, 16)
            for g in range(NG):
                act.dma_start(wrv[:, :, NG + g * EG:NG + (g + 1) * EG],
                              a["w_fine"][0, g].rearrange("(k p) e -> p k e", p=P)).then_inc(s_rp, 16)
            act.dma_start(rbias[:, 0:NG], a["b_coarse"].to_broadcast([P, NG])).then_inc(s_rp, 16)
            act.dma_start(rbias[:, NG:NG + NE],
                          a["b_fine"].rearrange("l g e -> l (g e)").to_broadcast([P, NE])).then_inc(s_rp, 16)

            def rms(at, n, t, squared, done):
                act.wait_ge(squared, t + 1)
                nc.scalar.activation(small[0:n, at + 24 + t:at + 25 + t], small[0:n, at + t:at + t + 1], ACT.Sqrt,
                                     scale=1.0 / D, bias=eps_rms[0:n, :]).then_inc(done, 1)

            act.wait_ge(s_const, NCON)
            for t in range(NT):
                act.wait_ge(s_x[t], 16)
                if t:
                    act.wait_ge(s_sq1, t)
                n = TROWS[t]
                nc.scalar.activation(sqj[0:n, :], x_in[0:n, t, :], ACT.Square,
                                     accum_out=small[0:n, t:t + 1]).then_inc(s_sq1, 1)
                rms(0, n, t, s_sq1, s_rms1)

            def evac(i, bank, dst, func):
                act.wait_ge(s_chunk, i + 1)
                for j in range(2):
                    ins = nc.scalar.activation(dst[:, j * HALF:(j + 1) * HALF], ps[2 * bank + j][:, 0:HALF], func)
                ins.then_inc(s_evac, 1)

            act.wait_ge(s_xn, NT)
            for c in range(CC):
                if c:
                    act.wait_ge(s_ub, c)
                evac(2 * c, 0, st[0], ACT.Copy)
                evac(2 * c + 1, 1, st[1], ACT.Sigmoid)
            act.dma_start(y_dram[NE * T:NBLK * T, :].rearrange("(b r) (h d) -> (r h) b d", r=T, h=2),
                          zeros[:, :].unsqueeze(1).to_broadcast([P, NBLK - NE, D // 2])).then_inc(s_yst, 16)

            for c in range(CC):
                if c:
                    act.wait_ge(s_ua, c)
                evac(2 * CC + 3 * c, 0, st[2], ACT.Copy)
                evac(2 * CC + 3 * c + 1, 1, st[3], ACT.Copy)
                if c:
                    act.wait_ge(s_za, c)
                evac(2 * CC + 3 * c + 2, 2, st[4], ACT.Copy)
                if c == 2:
                    act.wait_ge(s_histc, 2)
                    for k in range(CC):
                        act.wait_ge(s_dev, k + 1)
                        nc.scalar.activation(sq[:, k, :], z[:, CC + k, :], ACT.Square).then_inc(s_sqb, 1)
            act.wait_ge(s_var, 1)
            for j in range(2):
                ins = nc.scalar.activation(rs[:, j * HALF:(j + 1) * HALF], ps[6 + j][:, 0:HALF], ACT.Sqrt, bias=eps_ln)
            ins.then_inc(s_lnsd, 1)
            for k in range(CC):
                act.wait_ge(s_zn, k + 1)
                nc.scalar.activation(z[:, CC + k, :], z[:, CC + k, :], ACT.Silu,
                                     scale=parv[:, k, KB + KA + 1:KB + KA + 2],
                                     bias=parv[:, k, KB + KA + 2:KB + KA + 3]).then_inc(s_zb, 1)
            act.wait_ge(s_histc, 4)
            act.dma_start(nb_p[0, 0], st_p[0:HB, :]).then_inc(s_hout, 16)
            act.dma_start(na_s[0].rearrange("s j c -> (s j) c"), st_p[32:32 + NS * HA, :]).then_inc(s_hout, 16)
            act.dma_start(na_p[0, 0], st_p[64:64 + HA, :]).then_inc(s_hout, 16)
            nbs = nb_s[0].rearrange("s j c -> (s j) c")
            for i in range(2):
                act.dma_start(nbs[i * QR:(i + 1) * QR, :], st_b[0:QR, i * DA:(i + 1) * DA]).then_inc(s_hout, 16)
            act.wait_ge(s_var, 1)
            act.dma_start(gffn, a["g_ffn"].to_broadcast([P, D])).then_inc(s_gf, 16)
            act.dma_start(gfin, a["g_final"].rearrange("(l d) -> l d", l=1).to_broadcast([P, D])).then_inc(s_gfin, 16)

            for t in range(NT):
                n = TROWS[t]
                act.wait_ge(s_x1, t + 1)
                if t:
                    act.wait_ge(s_sq2, t)
                nc.scalar.activation(sq2[0:n, :], x1[0:n, t, :], ACT.Square,
                                     accum_out=small[0:n, 8 + t:9 + t]).then_inc(s_sq2, 1)
                rms(8, n, t, s_sq2, s_rms2)
                act.wait_ge(s_h2, t + 1)
                act.dma_start(h2_dram[t * P:t * P + n, :], h2[0:n, t % 2, :]).then_inc(s_h2d[t % 2], 16)
                act.wait_ge(s_h2t, t + 1)
                for j in range(2):
                    ins = nc.scalar.activation(h2T[:, t % 2, 4 * j:4 * j + 4, 0:n],
                                               ps[4 + j][:, 0:4 * n].rearrange("p (k n) -> p k n", k=4), ACT.Copy)
                ins.then_inc(s_h2T, 1)

            act.wait_ge(s_mask, 1)
            nc.scalar.activation(e4, e4, ACT.Exp).then_inc(s_ex, 1)
            nc.scalar.activation(dlt, dlt, ACT.Exp).then_inc(s_ex, 1)

            act.wait_ge(s_tab, 1)
            act.wait_ge(s_yst, 16)
            nblk = act.value_load(bound[0:1, NE:NE + 1], min_val=NE, max_val=NBLK)
            act.wait_ge(s_xt_ps, 1)
            nc.scalar.activation(xT[:, :, :].rearrange("p k n -> p (k n)"), ps[0][:, :], ACT.Copy).then_inc(s_xt, 1)
            with act.Fori(0, nblk) as g:
                act.wait_ge(s_gu, g + 1)
                nc.scalar.activation(sg_m, ps[1][:, 0:P], ACT.Silu).then_inc(s_silu, 1)
                act.wait_ge(s_xt_ps, g + 2)
                nc.scalar.activation(xT[:, :, :].rearrange("p k n -> p (k n)"), ps[0][:, :], ACT.Copy).then_inc(s_xt, 1)
                act.wait_ge(s_down, g + 1)
                act.wait_ge(s_yst, g * 32 + 16)
                nc.scalar.activation(yblk, ps[3][:, :], ACT.Copy).then_inc(s_yc, 1)
                act.wait_ge(s_yc, g + 1)
                for h in range(2):
                    act.dma_start(y_dram[bass.ds(g * T, T), h * (D // 2):(h + 1) * (D // 2)],
                                  yblk[h * T:(h + 1) * T, :]).then_inc(s_yst, 16)

            for t in range(NT):
                n = TROWS[t]
                act.wait_ge(s_fin, 2 * t + 1)
                nc.scalar.activation(yg[0][t][0:n, :], x1[0:n, t, :], ACT.Square,
                                     accum_out=small[0:n, 16 + t:17 + t]).then_inc(s_sq3, 1)
                rms(16, n, t, s_sq3, s_rms3)
                act.wait_ge(s_fin, 2 * t + 2)
                dst = y_prompt[0, t * P:t * P + n, :] if t < NT - 1 else y_sample.rearrange("s l d -> (s l) d")
                act.dma_start(dst, x1[0:n, t, :]).then_inc(s_out, 16)
            act.wait_ge(s_hout, 16 * 5)
            act.wait_ge(s_out, 16 * NT)

        @block.gpsimd
        def _(pool):
            pool.memset(ident[:, :], 0.0).then_inc(s_const0, 1)
            pool.memset(before[:, :], 1.0).then_inc(s_const0, 1)
            pool.memset(lnmean[:, :], 1.0 / DA).then_inc(s_const, 1)
            pool.memset(onesb[:, :], 1.0).then_inc(s_const, 1)
            for c in range(CC):
                pool.memset(ub[:, c, 0:HB], 0.0).then_inc(s_const, 1)
                pool.memset(ua[:, c, 0:HA], 0.0).then_inc(s_const, 1)
            pool.memset(lg[:, :], 0.0).then_inc(s_const, 1)
            pool.memset(m8, -3.0e38).then_inc(s_const, 1)
            pool.memset(zeros[:, :], 0.0).then_inc(s_const, 1)
            pool.memset(carry, 0.0).then_inc(s_const, 1)
            pool.memset(eps_rms, RMS_EPS).then_inc(s_const, 1)
            pool.memset(eps_ln, LN_EPS).then_inc(s_const, 1)
            for v, pat, base, mul in ((iota32, [[1, NE]], 0, 0), (iotaq, [[1, NIDX]], 0, 0), (iotar, [[1, T]], 0, 0),
                                      (thr, [[T, NTHR]], T, 0), (tokf, [[P, NT]], 0, 1)):
                pool.iota(v, pattern=pat, base=base, channel_multiplier=mul,
                          allow_small_or_imprecise_dtypes=True).then_inc(s_const, 1)
            pool.wait_ge(s_const0, 2)
            pool.affine_select(out=ident[:, :], in_=ident[:, :], compare_op=ALU.not_equal, fill=1.0,
                               base=0, pattern=[[-1, P]], channel_multiplier=1).then_inc(s_const, 1)
            pool.affine_select(out=before[:, :], in_=before[:, :], compare_op=ALU.is_gt, fill=0.0,
                               base=0, pattern=[[1, P]], channel_multiplier=-1).then_inc(s_const, 1)

            pool.wait_ge(s_hist, 1)
            for c in range(CC):
                pool.wait_ge(s_evac, 2 * c + 2)
                sv = st[0]
                sg = st[1]
                pool.tensor_tensor(ub[:, c, HB:HB + SEQ], sv[:, 0:SEQ], sg[:, 0:SEQ], ALU.mult)
                pool.tensor_tensor(sample(ub[:, c, :], SB, WB, HB, SL),
                                   sv[:, SEQ:NTOK].rearrange("p (s l) -> p s l", s=NS),
                                   sg[:, SEQ:NTOK].rearrange("p (s l) -> p s l", s=NS), ALU.mult).then_inc(s_ub, 1)

                pool.wait_ge(s_ub, c + 1)
                pool.tensor_copy(hist_b[:, c, :].rearrange("p (s j) -> p s j", s=NS),
                                 sample(ub[:, c, :], SB, WB, SL, HB)).then_inc(s_packb, 1)

            n3 = UA - HA
            for c in range(CC):
                pool.wait_ge(s_evac, 2 * CC + 3 * c + 2)
                pool.tensor_tensor(ua[:, c, HA:HA + SEQ], st[2][:, 0:SEQ], st[3][:, 0:SEQ], ALU.mult)
                pool.tensor_tensor(sample(ua[:, c, :], SA, WA, HA, SL),
                                   st[2][:, SEQ:NTOK].rearrange("p (s l) -> p s l", s=NS),
                                   st[3][:, SEQ:NTOK].rearrange("p (s l) -> p s l", s=NS), ALU.mult).then_inc(s_ua, 1)
                pool.wait_ge(s_ua, c + 1)
                pool.tensor_copy(hist_a[:, c, :].rearrange("p (s j) -> p s j", s=NS),
                                 sample(ua[:, c, :], SA, WA, SL, HA)).then_inc(s_packa, 1)
                base = 5 * c
                if c:
                    pool.wait_ge(s_za, c)
                pool.tensor_scalar(tA[:, 0:n3], ua[:, c, 0:n3], wA(c, 0), None, ALU.mult).then_inc(s_pa, 1)
                pool.tensor_scalar(tB[:, 0:n3], ua[:, c, 1:1 + n3], wA(c, 1), None, ALU.mult).then_inc(s_pa, 1)
                pool.wait_ge(s_pa, base + 2)
                pool.tensor_tensor(tA[:, 0:n3], tA[:, 0:n3], tB[:, 0:n3], ALU.add).then_inc(s_pa, 1)
                pool.wait_ge(s_pa, base + 3)
                pool.tensor_scalar(tB[:, 0:n3], ua[:, c, 2:2 + n3], wA(c, 2), None, ALU.mult).then_inc(s_pa, 1)
                pool.wait_ge(s_pa, base + 4)
                pool.tensor_tensor(tA[:, 0:n3], tA[:, 0:n3], tB[:, 0:n3], ALU.add).then_inc(s_pa, 1)
                pool.wait_ge(s_pa, base + 5)
                pool.wait_ge(s_evac, 2 * CC + 3 * c + 3)
                pool.tensor_tensor(z[:, c, 0:SEQ], tA[:, 0:SEQ], st[4][:, 0:SEQ], ALU.mult)
                pool.tensor_tensor(z[:, c, SEQ:NTOK].rearrange("p (s l) -> p s l", s=NS),
                                   tA[:, SA:SA + NS * WA].rearrange("p (s w) -> p s w", s=NS)[:, :, 0:SL],
                                   st[4][:, SEQ:NTOK].rearrange("p (s l) -> p s l", s=NS), ALU.mult).then_inc(s_za, 1)

            pool.wait_ge(s_tab, 1)
            for i in range(2):
                pool.wait_ge(s_h2d[i], 16 * ((NT + 1 - i) // 2))
            nblk = pool.value_load(bound[0:1, NE:NE + 1], min_val=NE, max_val=NBLK)

            def gather():
                pool.indirect_dma_start(xrow, None, h2_dram[:, :],
                                        bass.IndirectOffsetOnAxis(ap=idxcol[:, 0:1], axis=0)).then_inc(s_gath, 16)

            pool.tensor_copy(idxcol[:, :], inv_u[:, 0:1]).then_inc(s_idx, 1)
            pool.wait_ge(s_idx, 1)
            gather()
            with pool.Fori(0, nblk) as g:
                pool.wait_ge(s_xt_ps, g + 1)
                pool.tensor_copy(idxcol[:, :], inv_u[:, bass.ds(g + 1, 1)]).then_inc(s_idx, 1)
                pool.wait_ge(s_idx, g + 2)
                pool.tensor_tensor(carry[:, 0:1], carry[:, 1:2], carry[:, 1:2], ALU.add)
                gather()

            pool.wait_ge(s_yst, nblk * 32 + 16)
            pool.tensor_tensor(carry[:, 2:3], carry[:, 1:2], carry[:, 1:2], ALU.add)
            for t in range(NT):
                n = TROWS[t]
                for k in range(2):
                    pool.indirect_dma_start(yg[k][t][0:n, :], None, y_dram[:, :],
                                            bass.IndirectOffsetOnAxis(ap=rtu[0:n, k * NT + t:k * NT + t + 1], axis=0))\
                        .then_inc(s_yg[t], 16)

        @block.vector
        def _(dve):
            done = [0]

            def link(ins):
                done[0] += 1
                ins.then_inc(s_dve, 1)
                dve.wait_ge(s_dve, done[0])

            dve.wait_ge(s_const, NCON)
            dve.wait_ge(s_pT, 1)
            link(nc.vector.tensor_copy(par[:, :], ps[6][:, 0:CC * NP]))
            nc.vector.tensor_copy(gmix[:, :], ps[6][:, CC * NP:CC * NP + KC])
            for c in range(CC):
                nc.vector.tensor_copy(sample(ua[:, c, :], SA, WA, 0, HA),
                                      ps[6][:, 256 + c * NS * HA:256 + (c + 1) * NS * HA].rearrange("p (s j) -> p s j", s=NS))
                link(nc.vector.tensor_copy(sample(ub[:, c, :], SB, WB, 0, HB),
                                           ps[4 + c // 2][:, (c % 2) * NS * HB:(c % 2 + 1) * NS * HB]
                                           .rearrange("p (s j) -> p s j", s=NS)))
            nc.vector.memset(onesc, 1.0).then_inc(s_hist, 1)
            dve.wait_ge(s_hist, 1)

            def rstd(at, n, t):
                c = small[0:n, at + 24 + t:at + 25 + t]
                link(nc.vector.reciprocal(c, c))

            def norm_in(t):
                n = TROWS[t]
                dve.wait_ge(s_rms1, t + 1)
                rstd(0, n, t)
                if t >= 2:
                    dve.wait_ge(s_xT, t - 1)
                nc.vector.tensor_scalar(xn[0:n, t % 2, :], x_in[0:n, t, :], small[0:n, 24 + t:25 + t], None,
                                        ALU.mult).then_inc(s_xn, 1)

            def gain_in(t):
                n = TROWS[t]
                dve.wait_ge(s_xT, t + 1)
                for j in range(2):
                    ins = nc.vector.tensor_tensor(hT[:, 4 * j:4 * j + 4, t * P:t * P + n],
                                                  ps[2 * (t % 2) + j][:, 0:4 * n].rearrange("p (k n) -> p k n", k=4),
                                                  gmix[:, 4 * j:4 * j + 4].unsqueeze(2).to_broadcast([P, 4, n]), ALU.mult)
                ins.then_inc(s_hT, 1)

            for t in range(NT + 1):
                if t < NT:
                    norm_in(t)
                if t:
                    gain_in(t - 1)

            with nc.vector.Fori(0, CC) as c:
                uc = ub[:, bass.ds(c, 1), :].rearrange("p c n -> p (c n)")
                zc = z[:, bass.ds(c + CC, 1), :].rearrange("p c n -> p (c n)")
                pc = parv[:, bass.ds(c, 1), :].rearrange("p c n -> p (c n)")
                dve.wait_ge(s_ub, c + 1)
                zs = zc[:, SEQ:NTOK].rearrange("p (s l) -> p s l", s=NS)
                for j in range(KB):
                    up = uc[:, j:j + SEQ]
                    us = sample(uc, SB, WB, j, SL)
                    if j == 0:
                        b = pc[:, KB + KA:KB + KA + 1]
                        nc.vector.tensor_scalar(zc[:, 0:SEQ], up, pc[:, 0:1], b, ALU.mult, ALU.add).then_inc(s_conv, 1)
                        nc.vector.tensor_scalar(zs, us, pc[:, 0:1], b, ALU.mult, ALU.add).then_inc(s_conv, 1)
                        continue
                    dve.wait_ge(s_conv, c * (2 * KB) + 2 * j - 1)
                    nc.vector.scalar_tensor_tensor(out=zc[:, 0:SEQ], in0=up, scalar=pc[:, j:j + 1], in1=zc[:, 0:SEQ],
                                                   op0=ALU.mult, op1=ALU.add).then_inc(s_conv, 1)
                    dve.wait_ge(s_conv, c * (2 * KB) + 2 * j)
                    nc.vector.scalar_tensor_tensor(out=zs, in0=us, scalar=pc[:, j:j + 1], in1=zs,
                                                   op0=ALU.mult, op1=ALU.add).then_inc(s_conv, 1)
            dve.wait_ge(s_conv, CC * 2 * KB)
            nc.vector.memset(onesc, 1.0).then_inc(s_cb, 1)
            dve.wait_ge(s_hist, 2)
            nc.vector.tensor_copy(st_p[0:HB, :], ps[6][0:HB, :]).then_inc(s_histc, 1)
            dve.wait_ge(s_hist, 3)
            QR = NS * HB // 2
            nc.vector.tensor_copy(st_b[0:QR, 0:DA], ps[7][0:QR, :])
            dve.wait_ge(s_hist, 4)
            nc.vector.tensor_copy(st_b[0:QR, DA:2 * DA], ps[6][0:QR, :]).then_inc(s_histc, 1)

            dve.wait_ge(s_mu, 1)
            for k in range(CC):
                for j in range(2):
                    zz = z[:, CC + k, j * HALF:(j + 1) * HALF]
                    ins = nc.vector.tensor_tensor(zz, zz, ps[6 + j][:, 0:HALF], ALU.subtract)
                ins.then_inc(s_dev, 1)
            dve.wait_ge(s_var, 1)
            dve.wait_ge(s_lnsd, 1)
            link(nc.vector.reciprocal(rs, rs))
            for k in range(CC):
                nc.vector.tensor_tensor(z[:, CC + k, :], z[:, CC + k, :], rs, ALU.mult).then_inc(s_zn, 1)
            dve.wait_ge(s_hist, 5)
            nc.vector.tensor_copy(st_p[64:64 + HA, :], ps[6][0:HA, :]).then_inc(s_histc, 1)
            dve.wait_ge(s_hist, 6)
            nc.vector.tensor_copy(st_p[32:32 + NS * HA, :], ps[7][0:NS * HA, :]).then_inc(s_histc, 1)

            dve.wait_ge(s_xr, 16 * NT)
            dve.wait_ge(s_rp, 16 * (NG + 3))
            dve.wait_ge(s_gf, 16)

            def logits(t):
                n = TROWS[t]
                dve.wait_ge(s_lg, t + 1)
                nc.vector.tensor_tensor(lgv[0:n, t, :], ps[6 + t % 2][0:n, 0:NG + NE], rbias[0:n, :], ALU.add).then_inc(s_lgc, 1)

            for t in range(NT):
                n = TROWS[t]
                dve.wait_ge(s_o, t + 1)
                for j in range(2):
                    xh = x1[0:n, t, j * 512:(j + 1) * 512]
                    ins = nc.vector.tensor_tensor(xh, xh, ps[2 * (t % 2) + j][0:n, :], ALU.add)
                ins.then_inc(s_x1, 1)
                dve.wait_ge(s_rms2, t + 1)
                rstd(8, n, t)
                if t >= 2:
                    dve.wait_ge(s_h2d[t % 2], 16 * (t // 2))
                    dve.wait_ge(s_h2t, t - 1)
                nc.vector.scalar_tensor_tensor(out=h2[0:n, t % 2, :], in0=x1[0:n, t, :], scalar=small[0:n, 32 + t:33 + t],
                                               in1=gffn[0:n, :], op0=ALU.mult, op1=ALU.mult).then_inc(s_h2, 1)
                if t:
                    logits(t - 1)
            logits(NT - 1)
            dve.wait_ge(s_lgc, NT)

            for t in range(NT):
                link(nc.vector.tensor_copy(m8[:, 0:NG], lgv[:, t, 0:NG]))
                v = v8[:, 8 * t:8 * t + 8]
                link(nc.vector.max(v, m8))
                link(nc.vector.max_index(rtu[:, 32 + 8 * t:40 + 8 * t], v, m8))
                link(nc.vector.tensor_copy(grpf[:, t:t + 1], rtu[:, 32 + 8 * t:33 + 8 * t]))
                link(nc.vector.tensor_scalar(e4[:, NG * t:NG * t + NG], lgv[:, t, 0:NG], v[:, 0:1], None, ALU.subtract))
                link(nc.vector.tensor_scalar(oh4, iota32[:, 0:NG], grpf[:, t:t + 1], None, ALU.is_equal))
                fs = fsel[:, EG * t:EG * t + EG]
                link(nc.vector.tensor_scalar(fs, lgv[:, t, NG:NG + EG], oh4[:, 0:1], None, ALU.mult))
                for g in range(1, NG):
                    link(nc.vector.scalar_tensor_tensor(out=fs, in0=lgv[:, t, NG + g * EG:NG + (g + 1) * EG],
                                                        scalar=oh4[:, g:g + 1], in1=fs, op0=ALU.mult, op1=ALU.add))
                link(nc.vector.max(v, fs))
                link(nc.vector.max_index(rtu[:, 32 + 8 * t:40 + 8 * t], v, fs))
                link(nc.vector.tensor_tensor(dlt[:, t:t + 1], v[:, 1:2], v[:, 0:1], ALU.subtract))
                for k in range(2):
                    link(nc.vector.tensor_copy(ev[:, k * NT + t:k * NT + t + 1], rtu[:, 32 + 8 * t + k:33 + 8 * t + k]))
                    link(nc.vector.scalar_tensor_tensor(out=eid[:, k * NT + t:k * NT + t + 1], in0=grpf[:, t:t + 1],
                                                        scalar=float(EG), in1=ev[:, k * NT + t:k * NT + t + 1],
                                                        op0=ALU.mult, op1=ALU.add))
                for k in range(2):
                    link(nc.vector.tensor_scalar(m12[:, k * NE:(k + 1) * NE], iota32, eid[:, k * NT + t:k * NT + t + 1],
                                                 None, ALU.is_equal))
                link(nc.vector.tensor_tensor(maskb[:, t * NE:(t + 1) * NE], m12[:, 0:NE], m12[:, NE:2 * NE], ALU.add))
            nc.vector.memset(onesc, 1.0).then_inc(s_mask, 1)
            dve.wait_ge(s_ex, 2)
            link(nc.vector.tensor_reduce(pgr, e4.rearrange("p (t g) -> p t g", g=NG), AX.X, ALU.add))
            link(nc.vector.tensor_scalar(ngm, dlt, 1.0, None, ALU.add))
            link(nc.vector.tensor_tensor(pgr, pgr, ngm, ALU.mult))
            link(nc.vector.reciprocal(w12[:, 0:NT], pgr))
            link(nc.vector.tensor_tensor(w12[:, NT:2 * NT], w12[:, 0:NT], dlt, ALU.mult))

            dve.wait_ge(s_rank, 1)
            link(nc.vector.tensor_copy(cnt, ps[0][:, NT * NE:(NT + 1) * NE]))
            cv = cmp.rearrange("p (e h) -> p e h", h=NTHR)
            link(nc.vector.tensor_tensor(cv, cnt.unsqueeze(2).to_broadcast([P, NE, NTHR]),
                                         thr.unsqueeze(1).to_broadcast([P, NE, NTHR]), ALU.is_gt))
            link(nc.vector.tensor_reduce(nb, cv, AX.X, ALU.add))
            link(nc.vector.tensor_scalar(nb, nb, 1.0, None, ALU.add))
            src = nb
            for i, sh in enumerate((1, 2, 4, 8, 16)):
                dst = pfx[i % 2]
                link(nc.vector.tensor_copy(dst[:, 0:sh], src[:, 0:sh]))
                link(nc.vector.tensor_tensor(dst[:, sh:NE], src[:, sh:NE], src[:, 0:NE - sh], ALU.add))
                src = dst
            link(nc.vector.memset(bound[0:1, 0:1], 0))
            link(nc.vector.tensor_copy(bound[0:1, 1:NE + 1], src[0:1, :]))
            link(nc.vector.tensor_tensor(sbase, src, nb, ALU.subtract))
            link(nc.vector.tensor_scalar(sbase, sbase, float(T), None, ALU.mult))
            for t in range(NT):
                link(nc.vector.tensor_tensor(p32, sbase, ps[0][:, t * NE:(t + 1) * NE], ALU.add))
                for k in range(2):
                    i = k * NT + t
                    link(nc.vector.tensor_scalar(m12[:, k * NE:(k + 1) * NE], iota32, eid[:, i:i + 1], None, ALU.is_equal))
                    link(nc.vector.tensor_tensor(m12[:, k * NE:(k + 1) * NE], m12[:, k * NE:(k + 1) * NE], p32, ALU.mult))
                    link(nc.vector.tensor_reduce(slf[:, i:i + 1], m12[:, k * NE:(k + 1) * NE], AX.X, ALU.add))
            link(nc.vector.tensor_copy(rtu[:, 0:2 * NT], slf))
            link(nc.vector.tensor_copy(rti[:, 0:2 * NT], slf))
            link(nc.vector.tensor_scalar(rti[:, 16:16 + 2 * NT], rti[:, 0:2 * NT], 6, None, ALU.arith_shift_right))
            link(nc.vector.tensor_scalar(rti[:, 32:32 + 2 * NT], rti[:, 0:2 * NT], T - 1, None, ALU.bitwise_and))
            link(nc.vector.tensor_copy(qf, rti[:, 16:16 + 2 * NT]))
            link(nc.vector.tensor_copy(rf, rti[:, 32:32 + 2 * NT]))
            for i in range(2 * NT):
                k, t = divmod(i, NT)
                if i:
                    dve.wait_ge(s_inv, i)
                link(nc.vector.tensor_scalar(br_, iotar, rf[:, i:i + 1], None, ALU.is_equal))
                link(nc.vector.tensor_scalar(aq, iotaq, qf[:, i:i + 1], tokf[:, t:t + 1], ALU.is_equal, ALU.mult))
                nc.vector.memset(onesc, 1.0).then_inc(s_ab, 1)
            dve.wait_ge(s_inv, 2 * NT)
            nc.vector.tensor_copy(inv_u[:, :], ps[2][0:T, 0:NIDX]).then_inc(s_dve, 1)
            done[0] += 1
            dve.wait_ge(s_dve, done[0])
            nc.vector.memset(onesc, 1.0).then_inc(s_tab, 1)

            dve.wait_ge(s_tab, 1)
            nblk = dve.value_load(bound[0:1, NE:NE + 1], min_val=NE, max_val=NBLK)
            with nc.vector.Fori(0, nblk) as g:
                dve.wait_ge(s_silu, g + 1)
                nc.vector.tensor_tensor(hid, sg_m, ps[1][:, P:2 * P], ALU.mult).then_inc(s_hid, 1)
                dve.wait_ge(s_hT_ps, g + 1)
                nc.vector.tensor_copy(hidT, ps[2][:, 0:P]).then_inc(s_hidT, 1)

            dve.wait_ge(s_gfin, 16)
            for t in range(NT):
                n = TROWS[t]
                xt = x1[0:n, t, :]
                dve.wait_ge(s_yg[t], 32)
                for k in range(2):
                    link(nc.vector.scalar_tensor_tensor(out=xt, in0=yg[k][t][0:n, :], scalar=w12[0:n, k * NT + t:k * NT + t + 1],
                                                        in1=xt, op0=ALU.mult, op1=ALU.add))
                nc.vector.memset(onesc, 1.0).then_inc(s_fin, 1)
                dve.wait_ge(s_rms3, t + 1)
                rstd(16, n, t)
                nc.vector.scalar_tensor_tensor(out=xt, in0=xt, scalar=small[0:n, 40 + t:41 + t], in1=gfin[0:n, :],
                                               op0=ALU.mult, op1=ALU.mult).then_inc(s_fin, 1)

        @block.tensor
        def _(pe):
            mm = nc.tensor.matmul
            tr = nc.tensor.transpose
            pe.wait_ge(s_const, NCON)
            pe.wait_ge(s_par, 16 * 9)
            for c in range(CC):
                cs = slice(c * P, (c + 1) * P)
                tr(ps[6][:, c * NP:(c + 1) * NP], prow[:, cs], ident[0:NP, 0:NP])
                tr(ps[6][:, 256 + c * NS * HA:256 + (c + 1) * NS * HA], sa_rows[:, cs], ident[0:NS * HA, 0:NS * HA])
                QR = NS * HB // 2
                for i in range(2):
                    at = (c % 2) * NS * HB + i * QR
                    tr(ps[4 + c // 2][:, at:at + QR], sb_rows[0:QR, i * DA + c * P:i * DA + (c + 1) * P], ident[0:QR, 0:QR])
            tr(ps[6][:, CC * NP:CC * NP + KC], grow[:, :], ident[0:KC, 0:KC]).then_inc(s_pT, 1)

            for t in range(NT):
                n = TROWS[t]
                pe.wait_ge(s_xn, t + 1)
                if t >= 2:
                    pe.wait_ge(s_hT, t - 1)
                for k in range(KC):
                    ins = tr(ps[2 * (t % 2) + k // 4][:, (k % 4) * n:(k % 4 + 1) * n], xn[0:n, t % 2, k * P:(k + 1) * P],
                             ident[0:n, 0:n])
                ins.then_inc(s_xT, 1)

            def chunk(name, c, bank):
                for k in range(KC):
                    for j in range(2):
                        ins = mm(ps[2 * bank + j][:, 0:HALF], sec[name][:, k, c * P:(c + 1) * P],
                                 hT[:, k, j * HALF:(j + 1) * HALF], start=(k == 0), stop=(k == KC - 1))
                ins.then_inc(s_chunk, 1)

            pe.wait_ge(s_hT, NT)
            for c in range(CC):
                for i, name in enumerate(("vb", "gb")):
                    if c == 0:
                        pe.wait_ge(s_w[name], 16)
                    else:
                        pe.wait_ge(s_evac, 2 * c + i - 1)
                    chunk(name, c, i)

            def rows_out(bank, n, src):
                for c in range(CC):
                    ins = tr(ps[bank][0:n, c * P:(c + 1) * P], src(c), ident[:, :])
                ins.then_inc(s_hist, 1)

            for c in range(CC):
                for i, name in enumerate(("c", "va", "b")):
                    if c == 0:
                        pe.wait_ge(s_w[name], 16)
                        if i < 2:
                            pe.wait_ge(s_evac, 2 * CC - 1 + i)
                        else:
                            pe.wait_ge(s_hist, 1)
                    else:
                        pe.wait_ge(s_evac, 2 * CC + 3 * (c - 1) + i + 1)
                    chunk(name, c, i)
                    if (c, i) == (2, 0):
                        pe.wait_ge(s_packb, CC)
                        rows_out(6, HB, lambda c: ub[:, c, SEQ:SEQ + HB])
                        QR = NS * HB // 2
                        rows_out(7, QR, lambda c: hist_b[:, c, 0:QR])
                        pe.wait_ge(s_histc, 1)
                        rows_out(6, QR, lambda c: hist_b[:, c, QR:2 * QR])
                        pe.wait_ge(s_histc, 2)
                        pe.wait_ge(s_cb, 1)
                        for j in range(2):
                            for k in range(CC):
                                ins = mm(ps[6 + j][:, 0:HALF], lnmean[:, :], z[:, CC + k, j * HALF:(j + 1) * HALF],
                                         start=(k == 0), stop=(k == CC - 1))
                        ins.then_inc(s_mu, 1)
                    if (c, i) == (2, 2):
                        pe.wait_ge(s_sqb, CC)
                        for j in range(2):
                            for k in range(CC):
                                ins = mm(ps[6 + j][:, 0:HALF], lnmean[:, :], sq[:, k, j * HALF:(j + 1) * HALF],
                                         start=(k == 0), stop=(k == CC - 1))
                        ins.then_inc(s_var, 1)
            pe.wait_ge(s_zn, 1)
            pe.wait_ge(s_packa, CC)
            rows_out(6, HA, lambda c: ua[:, c, SEQ:SEQ + HA])
            rows_out(7, NS * HA, lambda c: hist_a[:, c, :])

            def route_tile(t):
                n = TROWS[t]
                pe.wait_ge(s_h2, t + 1)
                if t:
                    pe.wait_ge(s_h2T, t)
                for k in range(KC):
                    ins = tr(ps[4 + k // 4][:, (k % 4) * n:(k % 4 + 1) * n], h2[0:n, t % 2, k * P:(k + 1) * P], ident[0:n, 0:n])
                ins.then_inc(s_h2t, 1)
                pe.wait_ge(s_h2T, t + 1)
                if t >= 2:
                    pe.wait_ge(s_lgc, t - 1)
                elif t == 0:
                    pe.wait_ge(s_histc, 4)
                for k in range(KC):
                    ins = mm(ps[6 + t % 2][0:n, 0:NG + NE], h2T[:, t % 2, k, 0:n], wrv[:, k, :], start=(k == 0), stop=(k == KC - 1))
                ins.then_inc(s_lg, 1)

            pe.wait_ge(s_wout, 16)
            pe.wait_ge(s_za, CC)
            pe.wait_ge(s_zb, CC)
            pe.wait_ge(s_evac, 5 * CC)
            pe.wait_ge(s_rp, 16 * (NG + 3))
            for t in range(NT):
                n = TROWS[t]
                if t >= 2:
                    pe.wait_ge(s_x1, t - 1)
                for j in range(2):
                    for k in range(KC):
                        ins = mm(ps[2 * (t % 2) + j][0:n, :], z[:, k, t * P:t * P + n], w_out_sb[:, k, j * 512:(j + 1) * 512],
                                 start=(k == 0), stop=(k == KC - 1))
                ins.then_inc(s_o, 1)
                if t:
                    route_tile(t - 1)
            route_tile(NT - 1)

            pe.wait_ge(s_x1, NT)
            pe.wait_ge(s_mask, 1)
            for t in range(NT + 1):
                for u in range(min(t + 1, NT)):
                    n = TROWS[u]
                    ins = mm(ps[0][:, t * NE:(t + 1) * NE], (before if u == t else onesb)[0:n, :],
                             maskb[0:n, u * NE:(u + 1) * NE], start=(u == 0), stop=(u == min(t, NT - 1)))
            ins.then_inc(s_rank, 1)
            for i in range(2 * NT):
                n = TROWS[i % NT]
                pe.wait_ge(s_ab, i + 1)
                mm(ps[2][0:T, 0:NIDX], br_[0:n, :], aq[0:n, :], start=(i == 0), stop=(i == 2 * NT - 1)).then_inc(s_inv, 1)

            def tokens():
                for k in range(KC):
                    ins = tr(ps[0][:, k * T:(k + 1) * T], xrow[:, k * P:(k + 1) * P], ident[0:T, 0:T])
                ins.then_inc(s_xt_ps, 1)

            pe.wait_ge(s_tab, 1)
            pe.wait_ge(s_gath, 16)
            tokens()
            with pe.Fori(0, NE // NSLOT) as it:
                for i in range(NSLOT):
                    first = pe.value_load(bound[0:1, bass.ds(it * NSLOT + i, 1)], min_val=0, max_val=NBLK)
                    end = pe.value_load(bound[0:1, bass.ds(it * NSLOT + i + 1, 1)], min_val=1, max_val=NBLK)
                    half = KC * F
                    wgu = slot[i][:, 0:2 * half].rearrange("p (w k f) -> p k w f", w=2, k=KC)
                    wd = slot[i][:, 2 * half:WEXP].rearrange("p (c d) -> p c d", c=F // P)
                    with pe.Fori(first, end) as g:
                        pe.wait_ge(s_wexp[i], it * 48 + 48)
                        pe.wait_ge(s_xt, g + 1)
                        for k in range(KC):
                            for h in range(2):
                                ins = mm(ps[1][h * T:(h + 1) * T, 0:2 * P].rearrange("p (w f) -> p w f", w=2), xT[:, k, :],
                                         wgu[:, k, :, h * P:(h + 1) * P], start=(k == 0), stop=(k == KC - 1))
                        ins.then_inc(s_gu, 1)
                        pe.wait_ge(s_gath, g * 16 + 32)
                        mm(ps[5][0:32, 0:1], onesb[:, 0:32], onesb[:, 0:1], start=True, stop=True)
                        tokens()
                        pe.wait_ge(s_hid, g + 1)
                        tr(ps[2][:, 0:P], hid, ident[:, :]).then_inc(s_hT_ps, 1)
                        pe.wait_ge(s_hidT, g + 1)
                        for c in range(F // P):
                            for h in range(2):
                                ins = mm(ps[3][h * T:(h + 1) * T, :], hidT[:, c * T:(c + 1) * T], wd[:, c, h * 512:(h + 1) * 512],
                                         start=(c == 0), stop=(c == F // P - 1))
                        ins.then_inc(s_down, 1)


_INS = ["x_prompt", "x_sample", "state_conv_a", "state_conv_b", "g_mix", "w_in", "conv_a_w", "conv_b_w",
        "conv_b_bias", "ln_g", "ln_b", "w_out", "g_ffn", "w_coarse", "b_coarse", "w_fine", "b_fine",
        "w_gate", "w_up", "w_down", "g_final"]
_OUTS = [(1, SEQ, D), (NS, SL, D), (1, 1, HA, DA), (1, 1, HB, DA), (1, NS, HA, DA), (1, NS, HB, DA)]


def kernel(**inputs):
    import numpy as _np
    import concourse.bacc as _bacc
    from concourse import mybir as _mybir
    from concourse.bass_utils import run_bass_kernel_spmd as _run

    nc = _bacc.Bacc("TRN2", target_bir_lowering=False, num_devices=1)
    arrays, args, outs = {}, {}, []
    for name in _INS:
        v = _np.ascontiguousarray(inputs[name])
        arrays[f"in_{name}"] = v
        args[name] = nc.dram_tensor(f"in_{name}", v.shape, _mybir.dt.from_np(v.dtype), kind="ExternalInput").ap()
    for i, shape in enumerate(_OUTS):
        outs.append(nc.dram_tensor(f"out_{i}", shape, _mybir.dt.float32, kind="ExternalOutput").ap())
    build_step(nc, args, outs)
    r = _run(nc, [arrays], core_ids=[0])
    return tuple(r.results[0][f"out_{i}"] for i in range(len(_OUTS)))
```

```python
import concourse.bass as bass
from concourse import mybir
from contextlib import ExitStack

D = 1024
P = 128
KC = D // P
SEQ = 512
NS, SL = 8, 8
NTOK = SEQ + NS * SL
NT = (NTOK + P - 1) // P
TROWS = [min(P, NTOK - t * P) for t in range(NT)]
HALF = NTOK // 2
DA = 512
CC = DA // P
KA, KB = 3, 31
HA, HB = KA - 1, KB - 1
UA = HA + SEQ + NS * (HA + SL)
UB = HB + SEQ + NS * (HB + SL)
SA, SB = HA + SEQ, HB + SEQ
WA, WB = HA + SL, HB + SL
NG, EG = 4, 8
NE = NG * EG
F = 256
T = 64
NSLOT = 6
NBLK = NE + (2 * NTOK - 1) // T
NIDX = NBLK + 4
PAD = 2048
NTHR = (NTOK - 1) // T
QR = NS * HB // 2
RMS_EPS, LN_EPS = 1e-6, 1e-5


def build_step(nc, a, out):
    fp32, bf16 = mybir.dt.float32, mybir.dt.bfloat16
    i32, u32 = mybir.dt.int32, mybir.dt.uint32
    ALU = mybir.AluOpType
    ACT = mybir.ActivationFunctionType
    AX = mybir.AxisListType
    y_prompt, y_sample, na_p, nb_p, na_s, nb_s = out

    ctx = ExitStack()
    with ctx:
        def sb(name, shape, dt=fp32):
            return ctx.enter_context(nc.sbuf_tensor(name, shape, dt))

        def sem(name):
            return ctx.enter_context(nc.semaphore(name))

        h2_dram = nc.dram_tensor("h2_rows", (NTOK, D), fp32, kind="Internal").ap()
        y_dram = nc.dram_tensor("y_rows", (2 * NTOK, D), fp32, kind="Internal").ap()
        y_half = y_dram.rearrange("r (h d) -> (r h) d", h=2)

        PART = KC * F
        RX = sb("region_x", [P, NT * D])
        RH = sb("region_h", [P, NT * D])
        RW = sb("region_w", [P, 5 * KC * DA])
        SLOT0 = sb("slot0", [P, 3 * PART])
        ub_t = sb("ub", [P, CC * UB])
        ua_t = sb("ua", [P, CC * UA])
        z_t = sb("z", [P, KC * NTOK])

        x_in = RX[:, :].rearrange("p (t d) -> p t d", t=NT)
        hT = RH[:, 0:KC * NTOK].rearrange("p (k n) -> p k n", k=KC)
        x1 = RH[:, :].rearrange("p (t d) -> p t d", t=NT)
        SEC = KC * DA
        sec = {n: RW[:, i * SEC:(i + 1) * SEC].rearrange("p (k n) -> p k n", k=KC)
               for i, n in enumerate(["vb", "gb", "c", "va", "b"])}
        w_out_sb = RW[:, 0:2 * SEC].rearrange("p (k n) -> p k n", k=KC)
        places = [(SLOT0, 0, SLOT0, 2 * PART),
                  (RW, 2 * SEC, RW, 2 * SEC + 2 * PART), (RW, 2 * SEC + 3 * PART, RW, 2 * SEC + 5 * PART),
                  (RW, 0, RW, 2 * PART), (z_t, 0, RW, 3 * PART),
                  (RX, 0, ub_t, D)]
        slot_gu = [reg[:, lo:lo + 2 * PART] for reg, lo, _, _ in places]
        slot_dn = [reg[:, lo:lo + PART] for _, _, reg, lo in places]
        ub = ub_t[:, :].rearrange("p (c n) -> p c n", c=CC)
        ua = ua_t[:, :].rearrange("p (c n) -> p c n", c=CC)
        z = z_t[:, :].rearrange("p (c n) -> p c n", c=KC)
        xn = z_t[:, 0:2 * D].rearrange("p (b d) -> p b d", b=2)
        sqj = z_t[:, 2 * D:3 * D]
        st = [RX[:, i * NTOK:(i + 1) * NTOK] for i in range(5)]
        tA = RX[:, 5 * NTOK:5 * NTOK + UA]
        tB = RX[:, 5 * NTOK + UA:5 * NTOK + 2 * UA]
        rs = RX[:, 5 * NTOK + 2 * UA:6 * NTOK + 2 * UA]
        sq = ub_t[:, 0:CC * NTOK].rearrange("p (c n) -> p c n", c=CC)
        h2 = RX[:, 0:2 * D].rearrange("p (b d) -> p b d", b=2)
        h2T = RX[:, 2 * D:4 * D].rearrange("p (b k n) -> p b k n", b=2, k=KC)
        sq2 = RX[:, 4 * D:5 * D]
        gffn = ub_t[:, D:2 * D]
        gfin = ub_t[:, 0:D]
        stage = [RX[0:T, 2 * PART:2 * PART + D], RX[T:P, 2 * PART:2 * PART + D]]
        xT = z_t[:, 2 * PART:2 * PART + KC * T].rearrange("p (k n) -> p k n", k=KC)
        yblk = [ua_t[:, 3 * P + b * D // 2:3 * P + (b + 1) * D // 2] for b in range(2)]
        sg_m = ua_t[:, 0:P]
        hid = ua_t[:, P:2 * P]
        hidT = ua_t[:, 2 * P:3 * P]
        yg = [[(SLOT0 if k == 0 else RW)[:, t * D:(t + 1) * D] for t in range(NT)] for k in range(2)]

        ident = sb("ident", [P, P])
        lnmean = sb("lnmean", [P, P])
        before = sb("before", [P, P], bf16)
        onesb = sb("onesb", [P, P], bf16)
        pst = sb("pst", [P, DA])
        prow = pst[0:KB + KA + 3, :]
        grow = sb("grow", [KC, P])
        par = sb("par", [P, CC * (KB + KA + 3)])
        gmix = sb("gmix", [P, KC])
        sa_rows = sb("sa_rows", [NS * HA, DA])
        sb_rows = sb("sb_rows", [P, 2 * DA])
        st_b = sb_rows
        xrow = sb_rows[0:T, :]
        st_p = pst
        hist_b = sb("hist_b", [P, CC * NS * HB])[:, :].rearrange("p (c n) -> p c n", c=CC)
        hist_a = sb("hist_a", [P, CC * NS * HA])[:, :].rearrange("p (c n) -> p c n", c=CC)
        wr = sb("wr", [P, KC * (NG + NE)])
        rbias = sb("rbias", [P, NG + NE])
        small = sb("small", [P, 64])
        lg = sb("lg", [P, NT * (NG + NE)])
        RTW = 900
        rt = sb("rt", [P, RTW])
        rti = sb("rti", [P, 48], i32)
        rtu = sb("rtu", [P, 32 + 8 * NT], u32)
        maskb = sb("maskb", [P, NT * NE], bf16)
        gidx = sb("gidx", [T, NIDX], u32)
        sidx = sb("sidx", [P, NIDX], u32)
        gcol = sb("gcol", [T, 2], u32)
        scol = sb("scol", [P, 2], u32)
        bound = sb("bound", [1, NE + 4], i32)
        PAIRS, ODD, LASTP = NE + 1, NE + 2, NE + 3

        eps_rms, eps_ln = small[:, 60:61], small[:, 61:62]
        carry = sb("carry", [P, 4])[:, :]
        NCON = 20 + 2 * CC
        NP = KB + KA + 3
        parv = par[:, :].rearrange("p (c n) -> p c n", c=CC)

        def wB(c, j):
            return parv[:, c, j:j + 1]

        def wA(c, j):
            return parv[:, c, KB + j:KB + j + 1]

        ps = [ctx.enter_context(nc.psum_tensor(f"bank{i}", [P, 512], fp32)) for i in range(8)]

        s_x = [sem(f"s_xin{t}") for t in range(NT)]
        s_gmix = sem("s_gmix")
        s_par = sem("s_par")
        s_rp = sem("s_rp")
        s_w = {n: sem(f"s_w_{n}") for n in ["vb", "gb", "c", "va", "b"]}
        s_wout = sem("s_wout")
        s_xr = sem("s_xr")
        s_gf = sem("s_gf")
        s_gfin = sem("s_gfin")
        s_const = sem("s_const")
        s_const0 = sem("s_const0")
        s_sq1 = sem("s_sq1")
        s_rms1, s_rms2, s_rms3, s_lnsd = sem("s_rms1"), sem("s_rms2"), sem("s_rms3"), sem("s_lnsd")
        s_xn = sem("s_xn")
        s_xT = sem("s_xT")
        s_hT = sem("s_hT")
        s_gT = sem("s_gT")
        s_pT = sem("s_pT")
        s_pe_par = sem("s_pe_par")
        s_chunk = sem("s_chunk")
        s_evac = sem("s_evac")
        s_ub = sem("s_ub")
        s_uap = sem("s_uap")
        s_ua = sem("s_ua")
        s_za = sem("s_za")
        s_pa = sem("s_pa")
        s_conv = sem("s_conv")
        s_cb = sem("s_cb")
        s_mu = sem("s_mu")
        s_dev = sem("s_dev")
        s_sqb = sem("s_sqb")
        s_var = sem("s_var")
        s_zn = sem("s_zn")
        s_zb = sem("s_zb")
        s_hist = sem("s_hist")
        s_histc = sem("s_histc")
        s_packb = sem("s_packb")
        s_packa = sem("s_packa")
        s_hout = sem("s_hout")
        s_o = sem("s_o")
        s_x1 = sem("s_x1")
        s_sq2 = sem("s_sq2")
        s_h2 = sem("s_h2")
        s_h2d = [sem(f"s_h2d{i}") for i in range(2)]
        s_h2t = sem("s_h2t")
        s_h2T = sem("s_h2T")
        s_lg = sem("s_lg")
        s_lgc = sem("s_lgc")
        s_dve = sem("s_dve")
        s_ex = sem("s_ex")
        s_mask = sem("s_mask")
        s_rank = sem("s_rank")
        s_ab = sem("s_ab")
        s_inv = sem("s_inv")
        s_tab = sem("s_tab")
        s_route = sem("s_route")
        s_gi = sem("s_gi")
        s_si = sem("s_si")
        s_stage = sem("s_stage")
        s_gath = [sem(f"s_gath{b}") for b in range(2)]
        s_xt_ps = sem("s_xt_ps")
        s_xt = sem("s_xt")
        s_gu = sem("s_gu")
        s_silu = sem("s_silu")
        s_hid = sem("s_hid")
        s_hT_ps = sem("s_hT_ps")
        s_hidT = sem("s_hidT")
        s_down = sem("s_down")
        s_yc = sem("s_yc")
        s_ysc = [sem(f"s_ysc{b}") for b in range(2)]
        s_mv = sem("s_mv")
        s_wexp = [[sem(f"s_wexp{i}_{n}") for n in ("gate", "up", "down")] for i in range(NSLOT)]
        s_yg = [sem(f"s_yg{t}") for t in range(NT)]
        s_sq3 = sem("s_sq3")
        s_fin = sem("s_fin")
        s_out = sem("s_out")

        at = [0]

        def col(n):
            at[0] += n
            return rt[:, at[0] - n:at[0]]

        iota32, iotaq, iotar, thr = col(NE), col(NBLK), col(T), col(NTHR + 1)
        rowv = col(2 * NT)
        halfp = col(1)
        pgr, ngm, w12 = col(NT), col(NT), col(2 * NT)
        slf, nbn, sbase = col(2 * NT), col(NE), col(NE)
        pfx = [col(16 + NE), col(16 + NE)]
        m8, v8, grpf, g8 = col(8), col(8 * NT), col(NT), col(1)
        eid2 = col(2 * NT).rearrange("p (t k) -> p t k", k=2)
        e4, fsel, oh4, pick, dlt = col(NG * NT), col(EG * NT), col(NG), col(NE), col(NT)
        m1, mark = col(NE), col(2)
        vrow, vge = col(NBLK), col(NBLK)
        assert at[0] <= RTW
        xat = [0]

        def xcol(n):
            xat[0] += n
            return RX[:, 4 * D + xat[0] - n:4 * D + xat[0]]

        ohe, p32, cmp = xcol(2 * NT * NE), xcol(NT * NE), xcol(NE * (NTHR + 1))
        ohq = RX[:, 2 * D:2 * D + 2 * NT * NBLK].rearrange("p (i q) -> p i q", i=2 * NT)
        ohr = RX[:, 3 * D:3 * D + 2 * NT * T].rearrange("p (i r) -> p i r", i=2 * NT)

        lgv = lg[:, :].rearrange("p (t n) -> p t n", t=NT)
        wrv = wr[:, :].rearrange("p (k n) -> p k n", k=KC)

        def sample(ap, start, width, lo, n):
            return ap[:, start:start + NS * width].rearrange("p (s w) -> p s w", s=NS)[:, :, lo:lo + n]

        block = ctx.enter_context(nc.Block())

        @block.sync
        def _(sp):
            xp, xs = a["x_prompt"][0], a["x_sample"].rearrange("s l d -> (s l) d")

            def rows_of(t):
                return xp[t * P:(t + 1) * P, :] if t < NT - 1 else xs[:, :]

            def load_x(t):
                sp.dma_start(x_in[0:TROWS[t], t, :], rows_of(t)).then_inc(s_x[t], 16)

            load_x(0)
            load_x(1)
            sp.dma_start(grow[:, :], a["g_mix"][0].rearrange("(k p) -> k p", p=P)).then_inc(s_gmix, 16)
            r = 0
            for name, n in (("conv_b_w", KB), ("conv_a_w", KA)):
                sp.dma_start(prow[r:r + n, :], a[name][0]).then_inc(s_par, 16)
                r += n
            load_x(2)
            for name in ("conv_b_bias", "ln_g", "ln_b"):
                sp.dma_start(prow[r:r + 1, :], a[name]).then_inc(s_par, 16)
                r += 1
            load_x(3)
            sp.dma_start(sa_rows[:, :], a["state_conv_a"][0].rearrange("s j c -> (s j) c")).then_inc(s_par, 16)
            hb = a["state_conv_b"][0].rearrange("s j c -> (s j) c")
            for i in range(2):
                sp.dma_start(sb_rows[0:QR, i * DA:(i + 1) * DA], hb[i * QR:(i + 1) * QR, :]).then_inc(s_par, 16)
            load_x(4)
            cols = {"b": 0, "c": 1, "va": 2, "vb": 3, "gb": 4}
            w_in = a["w_in"][0].rearrange("(k p) n -> p k n", p=P)
            for n in ["vb", "gb", "c", "va", "b"]:
                sp.dma_start(sec[n], w_in[:, :, cols[n] * DA:(cols[n] + 1) * DA]).then_inc(s_w[n], 16)

            parts = ((a["w_gate"][0].rearrange("e (k p) f -> p e k f", p=P), KC),
                     (a["w_up"][0].rearrange("e (k p) f -> p e k f", p=P), KC),
                     (a["w_down"][0].rearrange("e (c p) d -> p e c d", p=P), F // P))

            def load_part(i, part, e):
                src, k = parts[part]
                dst = slot_dn[i] if part == 2 else slot_gu[i][:, part * PART:(part + 1) * PART]
                sp.dma_start(dst.rearrange("p (k f) -> p k f", k=k),
                             src[:, bass.ds(e, 1), :, :].rearrange("p e k f -> p (e k) f")).then_inc(s_wexp[i][part], 16)

            def load_expert(i, e):
                for part in range(3):
                    load_part(i, part, e)

            load_expert(0, 0)
            sp.wait_ge(s_chunk, 2 * CC)
            sp.dma_start(w_out_sb, a["w_out"][0].rearrange("(k p) n -> p k n", p=P)).then_inc(s_wout, 16)
            sp.wait_ge(s_chunk, 5 * CC)
            for t in range(NT):
                sp.dma_start(x1[0:TROWS[t], t, :], rows_of(t)).then_inc(s_xr, 16)
            load_expert(1, 1)
            load_expert(2, 2)
            sp.wait_ge(s_o, NT)
            load_expert(3, 3)
            load_expert(4, 4)
            sp.wait_ge(s_h2, NT)
            load_part(5, 2, 5)
            sp.wait_ge(s_tab, 1)
            for i in range(2):
                sp.wait_ge(s_h2d[i], 16 * ((NT + 1 - i) // 2))
            load_part(5, 0, 5)
            load_part(5, 1, 5)

            def reload(it, i):
                last = sp.value_load(bound[0:1, bass.ds(it * NSLOT + (i + 1 - NSLOT), 1)],
                                     min_val=1, max_val=NBLK)
                before_i, turn = (i - 1, it + 1) if i else (NSLOT - 1, it)
                for part in range(3):
                    if part < 2:
                        sp.wait_ge(s_wexp[before_i][part + 1], turn * 16)
                    else:
                        sp.wait_ge(s_wexp[i][0], it * 16 + 16)
                    if part == 0:
                        sp.wait_ge(s_down, last)
                    load_part(i, part, it * NSLOT + i)

            with sp.Fori(1, NE // NSLOT) as it:
                for i in range(NSLOT):
                    reload(it, i)
            for i in range(NE % NSLOT):
                reload(NE // NSLOT, i)
            pairs = sp.value_load(bound[0:1, PAIRS:PAIRS + 1], min_val=NE // 2, max_val=NBLK // 2)
            odd = sp.value_load(bound[0:1, ODD:ODD + 1], min_val=0, max_val=1)
            sp.wait_ge(s_ysc[1], pairs * 16)
            sp.wait_ge(s_ysc[0], (pairs + odd) * 16)
            for t in range(NT):
                for k in range(2):
                    sp.dma_start(yg[k][t][0:TROWS[t], :], y_dram[k * NTOK + t * P:k * NTOK + t * P + TROWS[t], :])\
                      .then_inc(s_yg[t], 16)

        @block.scalar
        def _(act):
            def rms(at, n, t, squared, done):
                act.wait_ge(squared, t + 1)
                nc.scalar.activation(small[0:n, at + 24 + t:at + 25 + t], small[0:n, at + t:at + t + 1], ACT.Sqrt,
                                     scale=1.0 / D, bias=eps_rms[0:n, :]).then_inc(done, 1)

            act.wait_ge(s_const, NCON)
            for t in range(NT):
                act.wait_ge(s_x[t], 16)
                if t:
                    act.wait_ge(s_sq1, t)
                n = TROWS[t]
                nc.scalar.activation(sqj[0:n, :], x_in[0:n, t, :], ACT.Square,
                                     accum_out=small[0:n, t:t + 1]).then_inc(s_sq1, 1)
                rms(0, n, t, s_sq1, s_rms1)

            def evac(i, bank, dst, func):
                act.wait_ge(s_chunk, i + 1)
                for j in range(2):
                    ins = nc.scalar.activation(dst[:, j * HALF:(j + 1) * HALF], ps[2 * bank + j][:, 0:HALF], func)
                ins.then_inc(s_evac, 1)

            act.dma_start(wrv[:, :, 0:NG], a["w_coarse"][0].rearrange("(k p) g -> p k g", p=P)).then_inc(s_rp, 16)
            for g in range(NG):
                act.dma_start(wrv[:, :, NG + g * EG:NG + (g + 1) * EG],
                              a["w_fine"][0, g].rearrange("(k p) e -> p k e", p=P)).then_inc(s_rp, 16)
            act.dma_start(rbias[:, 0:NG], a["b_coarse"].to_broadcast([P, NG])).then_inc(s_rp, 16)
            act.dma_start(rbias[:, NG:NG + NE],
                          a["b_fine"].rearrange("l g e -> l (g e)").to_broadcast([P, NE])).then_inc(s_rp, 16)

            act.wait_ge(s_xn, NT)
            for c in range(CC):
                if c:
                    act.wait_ge(s_ub, c)
                evac(2 * c, 0, st[0], ACT.Copy)
                evac(2 * c + 1, 1, st[1], ACT.Sigmoid)
            for c in range(CC):
                if c:
                    act.wait_ge(s_ua, c)
                evac(2 * CC + 3 * c, 0, st[2], ACT.Copy)
                evac(2 * CC + 3 * c + 1, 1, st[3], ACT.Copy)
                if c == 2:
                    act.wait_ge(s_hist, 3)
                    nc.scalar.activation(st_p[0:HB, :], ps[6][0:HB, :], ACT.Copy)
                    nc.scalar.activation(st_b[0:QR, 0:DA], ps[7][0:QR, :], ACT.Copy).then_inc(s_histc, 1)
                if c == 3:
                    for k in range(CC):
                        act.wait_ge(s_dev, k + 1)
                        nc.scalar.activation(sq[:, k, :], z[:, CC + k, :], ACT.Square).then_inc(s_sqb, 1)
                if c == 3:
                    act.wait_ge(s_var, 1)
                    for j in range(2):
                        ins = nc.scalar.activation(rs[:, j * HALF:(j + 1) * HALF], ps[6 + j][:, 0:HALF], ACT.Sqrt, bias=eps_ln)
                    ins.then_inc(s_lnsd, 1)
                if c == 3:
                    for k in range(CC):
                        act.wait_ge(s_zn, k + 1)
                        nc.scalar.activation(z[:, CC + k, :], z[:, CC + k, :], ACT.Silu,
                                             scale=parv[:, k, KB + KA + 1:KB + KA + 2],
                                             bias=parv[:, k, KB + KA + 2:KB + KA + 3]).then_inc(s_zb, 1)
                if c:
                    act.wait_ge(s_za, c)
                evac(2 * CC + 3 * c + 2, 2, st[4], ACT.Copy)
                if c == 2:
                    act.wait_ge(s_hist, 4)
                    nc.scalar.activation(st_b[0:QR, DA:2 * DA], ps[6][0:QR, :], ACT.Copy).then_inc(s_histc, 1)
            act.wait_ge(s_var, 1)
            act.dma_start(gffn, a["g_ffn"].to_broadcast([P, D])).then_inc(s_gf, 16)
            act.dma_start(gfin, a["g_final"].rearrange("(l d) -> l d", l=1).to_broadcast([P, D])).then_inc(s_gfin, 16)

            for t in range(NT):
                n = TROWS[t]
                act.wait_ge(s_x1, t + 1)
                if t:
                    act.wait_ge(s_sq2, t)
                nc.scalar.activation(sq2[0:n, :], x1[0:n, t, :], ACT.Square,
                                     accum_out=small[0:n, 8 + t:9 + t]).then_inc(s_sq2, 1)
                rms(8, n, t, s_sq2, s_rms2)
                act.wait_ge(s_h2, t + 1)
                act.dma_start(h2_dram[t * P:t * P + n, :], h2[0:n, t % 2, :]).then_inc(s_h2d[t % 2], 16)
                act.wait_ge(s_h2t, t + 1)
                for j in range(2):
                    ins = nc.scalar.activation(h2T[:, t % 2, 4 * j:4 * j + 4, 0:n],
                                               ps[4 + j][:, 0:4 * n].rearrange("p (k n) -> p k n", k=4), ACT.Copy)
                ins.then_inc(s_h2T, 1)

            act.wait_ge(s_histc, 4)
            act.dma_start(nb_p[0, 0], st_p[0:HB, :]).then_inc(s_hout, 16)
            act.dma_start(na_s[0].rearrange("s j c -> (s j) c"), st_p[32:32 + NS * HA, :]).then_inc(s_hout, 16)
            act.dma_start(na_p[0, 0], st_p[64:64 + HA, :]).then_inc(s_hout, 16)
            nbs = nb_s[0].rearrange("s j c -> (s j) c")
            for i in range(2):
                act.dma_start(nbs[i * QR:(i + 1) * QR, :], st_b[0:QR, i * DA:(i + 1) * DA]).then_inc(s_hout, 16)

            act.wait_ge(s_mask, 1)
            nc.scalar.activation(e4, e4, ACT.Exp).then_inc(s_ex, 1)
            nc.scalar.activation(dlt, dlt, ACT.Exp).then_inc(s_ex, 1)

            act.wait_ge(s_tab, 1)
            pairs = act.value_load(bound[0:1, PAIRS:PAIRS + 1], min_val=NE // 2, max_val=NBLK // 2)
            last_pair = act.value_load(bound[0:1, LASTP:LASTP + 1], min_val=NE // 2 - 1, max_val=NBLK // 2 - 1)
            odd = act.value_load(bound[0:1, ODD:ODD + 1], min_val=0, max_val=1)

            def tokens_out(n):
                act.wait_ge(s_xt_ps, n)
                nc.scalar.activation(xT[:, :, :].rearrange("p k n -> p (k n)"), ps[0][:, :], ACT.Copy).then_inc(s_xt, 1)

            def silu_gate(n):
                act.wait_ge(s_gu, n)
                nc.scalar.activation(sg_m, ps[1][:, 0:P], ACT.Silu).then_inc(s_silu, 1)

            def outputs_out(q, b):
                act.wait_ge(s_down, q * 2 + (b + 1))
                if not isinstance(q, int):
                    act.wait_ge(s_ysc[b], q * 16)
                nc.scalar.activation(yblk[b], ps[3][:, :], ACT.Copy).then_inc(s_yc, 1)

            tokens_out(1)
            for g in range(3):
                silu_gate(g + 1)
                tokens_out(g + 2)
                if g:
                    outputs_out(0, g - 1)
            with act.Fori(1, last_pair) as q:
                for b in range(2):
                    silu_gate(q * 2 + (b + 2))
                    tokens_out(q * 2 + (b + 3))
                    outputs_out(q, b)
            silu_gate(pairs * 2)
            tokens_out(pairs * 2 + 1)
            outputs_out(last_pair, 0)
            with act.If(odd > 0):
                silu_gate(pairs * 2 + 1)
                tokens_out(pairs * 2 + 2)
            outputs_out(last_pair, 1)
            with act.If(odd > 0):
                outputs_out(pairs, 0)

            for t in range(NT):
                n = TROWS[t]
                act.wait_ge(s_fin, 2 * t + 1)
                nc.scalar.activation(yg[0][t][0:n, :], x1[0:n, t, :], ACT.Square,
                                     accum_out=small[0:n, 16 + t:17 + t]).then_inc(s_sq3, 1)
                rms(16, n, t, s_sq3, s_rms3)
                act.wait_ge(s_fin, 2 * t + 2)
                dst = y_prompt[0, t * P:t * P + n, :] if t < NT - 1 else y_sample.rearrange("s l d -> (s l) d")
                act.dma_start(dst, x1[0:n, t, :]).then_inc(s_out, 16)
            act.wait_ge(s_hout, 16 * 5)
            act.wait_ge(s_out, 16 * NT)

        @block.gpsimd
        def _(pool):
            pool.memset(ident[:, :], 0.0).then_inc(s_const0, 1)
            pool.memset(before[:, :], 1.0).then_inc(s_const0, 1)
            pool.memset(halfp, 1.0).then_inc(s_const0, 1)
            pool.memset(lnmean[:, :], 1.0 / DA).then_inc(s_const, 1)
            pool.memset(onesb[:, :], 1.0).then_inc(s_const, 1)
            for c in range(CC):
                pool.memset(ub[:, c, 0:HB], 0.0).then_inc(s_const, 1)
                pool.memset(ua[:, c, 0:HA], 0.0).then_inc(s_const, 1)
            pool.memset(lg[:, :], 0.0).then_inc(s_const, 1)
            pool.memset(m8, -3.0e38).then_inc(s_const, 1)
            pool.memset(carry, 0.0).then_inc(s_const, 1)
            pool.memset(thr[:, 0:1], -1.0).then_inc(s_const, 1)
            for v in pfx:
                pool.memset(v[:, 0:16], 0.0).then_inc(s_const, 1)
            pool.memset(bound[0:1, 0:1], 0).then_inc(s_const, 1)
            pool.memset(gidx[:, NBLK:NIDX], PAD).then_inc(s_const, 1)
            pool.memset(eps_rms, RMS_EPS).then_inc(s_const, 1)
            pool.memset(eps_ln, LN_EPS).then_inc(s_const, 1)
            for v, pat, base, mul in ((iota32, [[1, NE]], 0, 0), (iotaq, [[1, NBLK]], 0, 0), (iotar, [[1, T]], 0, 0),
                                      (thr[:, 1:NTHR + 1], [[T, NTHR]], T, 0),
                                      (rowv, [[-NTOK, 2], [-P, NT]], PAD, -1)):
                pool.iota(v, pattern=pat, base=base, channel_multiplier=mul,
                          allow_small_or_imprecise_dtypes=True).then_inc(s_const, 1)
            pool.wait_ge(s_const0, 3)
            pool.affine_select(out=ident[:, :], in_=ident[:, :], compare_op=ALU.not_equal, fill=1.0,
                               base=0, pattern=[[-1, P]], channel_multiplier=1).then_inc(s_const, 1)
            pool.affine_select(out=before[:, :], in_=before[:, :], compare_op=ALU.is_gt, fill=0.0,
                               base=0, pattern=[[1, P]], channel_multiplier=-1).then_inc(s_const, 1)

            pool.affine_select(out=halfp, in_=halfp, compare_op=ALU.is_ge, fill=0.0,
                               base=-T, pattern=[[0, 1]], channel_multiplier=1).then_inc(s_const, 1)

            pool.wait_ge(s_hist, 1)
            for c in range(CC):
                pool.wait_ge(s_evac, 2 * c + 2)
                sv = st[0]
                sg = st[1]
                pool.tensor_tensor(ub[:, c, HB:HB + SEQ], sv[:, 0:SEQ], sg[:, 0:SEQ], ALU.mult)
                pool.tensor_tensor(sample(ub[:, c, :], SB, WB, HB, SL),
                                   sv[:, SEQ:NTOK].rearrange("p (s l) -> p s l", s=NS),
                                   sg[:, SEQ:NTOK].rearrange("p (s l) -> p s l", s=NS), ALU.mult).then_inc(s_ub, 1)

                pool.wait_ge(s_ub, c + 1)
                pool.tensor_copy(hist_b[:, c, :].rearrange("p (s j) -> p s j", s=NS),
                                 sample(ub[:, c, :], SB, WB, SL, HB)).then_inc(s_packb, 1)

            n3 = UA - HA
            for c in range(CC):
                pool.wait_ge(s_evac, 2 * CC + 3 * c + 2)
                pool.tensor_tensor(ua[:, c, HA:HA + SEQ], st[2][:, 0:SEQ], st[3][:, 0:SEQ], ALU.mult)
                pool.tensor_tensor(sample(ua[:, c, :], SA, WA, HA, SL),
                                   st[2][:, SEQ:NTOK].rearrange("p (s l) -> p s l", s=NS),
                                   st[3][:, SEQ:NTOK].rearrange("p (s l) -> p s l", s=NS), ALU.mult).then_inc(s_ua, 1)
                pool.wait_ge(s_ua, c + 1)
                pool.tensor_copy(hist_a[:, c, :].rearrange("p (s j) -> p s j", s=NS),
                                 sample(ua[:, c, :], SA, WA, SL, HA)).then_inc(s_packa, 1)
                base = 5 * c
                if c:
                    pool.wait_ge(s_za, c)
                pool.tensor_scalar(tA[:, 0:n3], ua[:, c, 0:n3], wA(c, 0), None, ALU.mult).then_inc(s_pa, 1)
                pool.tensor_scalar(tB[:, 0:n3], ua[:, c, 1:1 + n3], wA(c, 1), None, ALU.mult).then_inc(s_pa, 1)
                pool.wait_ge(s_pa, base + 2)
                pool.tensor_tensor(tA[:, 0:n3], tA[:, 0:n3], tB[:, 0:n3], ALU.add).then_inc(s_pa, 1)
                pool.wait_ge(s_pa, base + 3)
                pool.tensor_scalar(tB[:, 0:n3], ua[:, c, 2:2 + n3], wA(c, 2), None, ALU.mult).then_inc(s_pa, 1)
                pool.wait_ge(s_pa, base + 4)
                pool.tensor_tensor(tA[:, 0:n3], tA[:, 0:n3], tB[:, 0:n3], ALU.add).then_inc(s_pa, 1)
                pool.wait_ge(s_pa, base + 5)
                pool.wait_ge(s_evac, 2 * CC + 3 * c + 3)
                pool.tensor_tensor(z[:, c, 0:SEQ], tA[:, 0:SEQ], st[4][:, 0:SEQ], ALU.mult)
                pool.tensor_tensor(z[:, c, SEQ:NTOK].rearrange("p (s l) -> p s l", s=NS),
                                   tA[:, SA:SA + NS * WA].rearrange("p (s w) -> p s w", s=NS)[:, :, 0:SL],
                                   st[4][:, SEQ:NTOK].rearrange("p (s l) -> p s l", s=NS), ALU.mult).then_inc(s_za, 1)

            pool.wait_ge(s_ab, 1)
            pool.memset(RX[:, 2 * PART:2 * PART + D], 0.0).then_inc(s_stage, 1)
            pool.wait_ge(s_tab, 1)
            pool.wait_ge(s_stage, 1)
            for i in range(2):
                pool.wait_ge(s_h2d[i], 16 * ((NT + 1 - i) // 2))
            pairs = pool.value_load(bound[0:1, PAIRS:PAIRS + 1], min_val=NE // 2, max_val=NBLK // 2)
            odd = pool.value_load(bound[0:1, ODD:ODD + 1], min_val=0, max_val=1)

            def gather(g, b):
                pool.tensor_copy(gcol[:, b:b + 1], gidx[:, bass.ds(g, 1)]).then_inc(s_gi, 1)
                pool.wait_ge(s_gi, g + 1)
                pool.tensor_tensor(carry[:, 0:1], carry[:, 1:2], carry[:, 1:2], ALU.add)
                pool.indirect_dma_start(stage[b], None, h2_dram[:, :], bass.IndirectOffsetOnAxis(ap=gcol[:, b:b + 1], axis=0),
                                        bounds_check=NTOK - 1, oob_is_err=False).then_inc(s_gath[b], 16)

            def scatter(g, b):
                pool.wait_ge(s_yc, g + 2)
                pool.tensor_copy(scol[:, b:b + 1], sidx[:, bass.ds(g, 1)]).then_inc(s_si, 1)
                pool.wait_ge(s_si, g + 1)
                pool.tensor_tensor(carry[:, 2:3], carry[:, 1:2], carry[:, 1:2], ALU.add)
                pool.indirect_dma_start(y_half, bass.IndirectOffsetOnAxis(ap=scol[:, b:b + 1], axis=0), yblk[b], None,
                                        bounds_check=4 * NTOK - 1, oob_is_err=False).then_inc(s_ysc[b], 16)

            gather(0, 0)
            gather(1, 1)
            for g in range(2, 4):
                pool.wait_ge(s_mv, g - 1)
                gather(g, g % 2)
            with pool.Fori(0, pairs) as h:
                for b in range(2):
                    pool.wait_ge(s_mv, h * 2 + (b + 3))
                    gather(h * 2 + (b + 4), b)
                    scatter(h * 2 + b, b)
            with pool.If(odd > 0):
                scatter(pairs * 2, 0)

        @block.vector
        def _(dve):
            done = [0]

            def link(ins):
                done[0] += 1
                ins.then_inc(s_dve, 1)
                dve.wait_ge(s_dve, done[0])

            dve.wait_ge(s_const, NCON)
            def rstd(at, n, t):
                c = small[0:n, at + 24 + t:at + 25 + t]
                link(nc.vector.reciprocal(c, c))

            def gain_in(t):
                n = TROWS[t]
                dve.wait_ge(s_xT, t + 1)
                for j in range(2):
                    ins = nc.vector.tensor_tensor(hT[:, 4 * j:4 * j + 4, t * P:t * P + n],
                                                  ps[2 * (t % 2) + j][:, 0:4 * n].rearrange("p (k n) -> p k n", k=4),
                                                  gmix[:, 4 * j:4 * j + 4].unsqueeze(2).to_broadcast([P, 4, n]), ALU.mult)
                ins.then_inc(s_hT, 1)

            def norm_in(t):
                n = TROWS[t]
                dve.wait_ge(s_rms1, t + 1)
                rstd(0, n, t)
                if t >= 2:
                    dve.wait_ge(s_xT, t - 1)
                nc.vector.tensor_scalar(xn[0:n, t % 2, :], x_in[0:n, t, :], small[0:n, 24 + t:25 + t], None,
                                        ALU.mult).then_inc(s_xn, 1)

            norm_in(0)
            dve.wait_ge(s_gT, 1)
            link(nc.vector.tensor_copy(gmix[:, :], ps[7][:, 0:KC]))
            for t in range(1, NT + 1):
                if t < NT:
                    norm_in(t)
                gain_in(t - 1)
            dve.wait_ge(s_pT, 1)
            link(nc.vector.tensor_copy(par[:, :], ps[6][:, 0:CC * NP]))
            for c in range(CC):
                nc.vector.tensor_copy(sample(ua[:, c, :], SA, WA, 0, HA),
                                      ps[6][:, 256 + c * NS * HA:256 + (c + 1) * NS * HA].rearrange("p (s j) -> p s j", s=NS))
                ins = nc.vector.tensor_copy(sample(ub[:, c, :], SB, WB, 0, HB),
                                            ps[4 + c // 2][:, (c % 2) * NS * HB:(c % 2 + 1) * NS * HB]
                                            .rearrange("p (s j) -> p s j", s=NS))
            ins.then_inc(s_hist, 1)
            dve.wait_ge(s_hist, 1)

            with nc.vector.Fori(0, CC) as c:
                uc = ub[:, bass.ds(c, 1), :].rearrange("p c n -> p (c n)")
                zc = z[:, bass.ds(c + CC, 1), :].rearrange("p c n -> p (c n)")
                pc = parv[:, bass.ds(c, 1), :].rearrange("p c n -> p (c n)")
                dve.wait_ge(s_ub, c + 1)
                zs = zc[:, SEQ:NTOK].rearrange("p (s l) -> p s l", s=NS)
                for j in range(KB):
                    up = uc[:, j:j + SEQ]
                    us = sample(uc, SB, WB, j, SL)
                    if j == 0:
                        b = pc[:, KB + KA:KB + KA + 1]
                        nc.vector.tensor_scalar(zc[:, 0:SEQ], up, pc[:, 0:1], b, ALU.mult, ALU.add).then_inc(s_conv, 1)
                        nc.vector.tensor_scalar(zs, us, pc[:, 0:1], b, ALU.mult, ALU.add).then_inc(s_conv, 1)
                        continue
                    dve.wait_ge(s_conv, c * (2 * KB) + 2 * j - 1)
                    nc.vector.scalar_tensor_tensor(out=zc[:, 0:SEQ], in0=up, scalar=pc[:, j:j + 1], in1=zc[:, 0:SEQ],
                                                   op0=ALU.mult, op1=ALU.add).then_inc(s_conv, 1)
                    dve.wait_ge(s_conv, c * (2 * KB) + 2 * j)
                    nc.vector.scalar_tensor_tensor(out=zs, in0=us, scalar=pc[:, j:j + 1], in1=zs,
                                                   op0=ALU.mult, op1=ALU.add).then_inc(s_conv, 1)
            dve.wait_ge(s_conv, CC * 2 * KB)
            nc.vector.memset(mark, 1.0).then_inc(s_cb, 1)
            dve.wait_ge(s_mu, 1)
            for k in range(CC):
                for j in range(2):
                    zz = z[:, CC + k, j * HALF:(j + 1) * HALF]
                    ins = nc.vector.tensor_tensor(zz, zz, ps[6 + j][:, 0:HALF], ALU.subtract)
                ins.then_inc(s_dev, 1)
            dve.wait_ge(s_var, 1)
            dve.wait_ge(s_lnsd, 1)
            link(nc.vector.reciprocal(rs, rs))
            for k in range(CC):
                nc.vector.tensor_tensor(z[:, CC + k, :], z[:, CC + k, :], rs, ALU.mult).then_inc(s_zn, 1)
            dve.wait_ge(s_xr, 16 * NT)
            dve.wait_ge(s_rp, 16 * (NG + 3))
            dve.wait_ge(s_gf, 16)

            def logits(t):
                n = TROWS[t]
                dve.wait_ge(s_lg, t + 1)
                nc.vector.tensor_tensor(lgv[0:n, t, :], ps[6 + t % 2][0:n, 0:NG + NE], rbias[0:n, :], ALU.add).then_inc(s_lgc, 1)

            def select(t):
                dve.wait_ge(s_lgc, t + 1)
                link(nc.vector.tensor_copy(m8[:, 0:NG], lgv[:, t, 0:NG]))
                v = v8[:, 8 * t:8 * t + 8]
                vi = rtu[:, 32 + 8 * t:40 + 8 * t]
                link(nc.vector.max(v, m8))
                nc.vector.tensor_scalar(e4[:, NG * t:NG * t + NG], lgv[:, t, 0:NG], v[:, 0:1], None, ALU.subtract)
                link(nc.vector.max_index(vi, v, m8))
                link(nc.vector.tensor_copy(grpf[:, t:t + 1], vi[:, 0:1]))
                nc.vector.tensor_scalar(g8, grpf[:, t:t + 1], float(EG), None, ALU.mult)
                link(nc.vector.tensor_scalar(oh4, iota32[:, 0:NG], grpf[:, t:t + 1], None, ALU.is_equal))
                fs = fsel[:, EG * t:EG * t + EG]
                link(nc.vector.tensor_tensor(pick.rearrange("p (g e) -> p g e", g=NG),
                                             lgv[:, t, NG:NG + NE].rearrange("p (g e) -> p g e", g=NG),
                                             oh4.unsqueeze(2).to_broadcast([P, NG, EG]), ALU.mult))
                link(nc.vector.tensor_reduce(fs, pick.rearrange("p (g e) -> p e g", g=NG), AX.X, ALU.add))
                link(nc.vector.max(v, fs))
                nc.vector.tensor_tensor(dlt[:, t:t + 1], v[:, 1:2], v[:, 0:1], ALU.subtract)
                link(nc.vector.max_index(vi, v, fs))
                link(nc.vector.tensor_scalar(eid2[:, t, :], vi[:, 0:2], g8, None, ALU.add))
                link(nc.vector.tensor_scalar(m1, iota32, eid2[:, t, 0:1], None, ALU.is_equal))
                ins = nc.vector.scalar_tensor_tensor(out=maskb[:, t * NE:(t + 1) * NE], in0=iota32, scalar=eid2[:, t, 1:2],
                                                     in1=m1, op0=ALU.is_equal, op1=ALU.add)
                if t == NT - 1:
                    ins.then_inc(s_mask, 1)
                else:
                    link(ins)

            for t in range(NT):
                n = TROWS[t]
                dve.wait_ge(s_o, t + 1)
                for j in range(2):
                    xh = x1[0:n, t, j * 512:(j + 1) * 512]
                    lo = 0 if n > T else j * T
                    ins = nc.vector.tensor_tensor(xh, xh, ps[2 * (t % 2) + j][lo:lo + n, :], ALU.add)
                ins.then_inc(s_x1, 1)
                dve.wait_ge(s_rms2, t + 1)
                rstd(8, n, t)
                if t >= 2:
                    dve.wait_ge(s_h2d[t % 2], 16 * (t // 2))
                    dve.wait_ge(s_h2t, t - 1)
                nc.vector.scalar_tensor_tensor(out=h2[0:n, t % 2, :], in0=x1[0:n, t, :], scalar=small[0:n, 32 + t:33 + t],
                                               in1=gffn[0:n, :], op0=ALU.mult, op1=ALU.mult).then_inc(s_h2, 1)
                if t == 0:
                    dve.wait_ge(s_hist, 5)
                    nc.vector.tensor_copy(st_p[64:64 + HA, :], ps[6][0:HA, :]).then_inc(s_histc, 1)
                    dve.wait_ge(s_hist, 6)
                    nc.vector.tensor_copy(st_p[32:32 + NS * HA, :], ps[7][0:NS * HA, :]).then_inc(s_histc, 1)
                else:
                    logits(t - 1)
                    select(t - 1)
            logits(NT - 1)
            select(NT - 1)

            dve.wait_ge(s_mask, 1)
            for k in range(2):
                ins = nc.vector.tensor_tensor(ohe[:, k * NT * NE:(k + 1) * NT * NE].rearrange("p (t e) -> p t e", t=NT),
                                              iota32.unsqueeze(1).to_broadcast([P, NT, NE]),
                                              eid2[:, :, k:k + 1].to_broadcast([P, NT, NE]), ALU.is_equal)
            link(ins)
            dve.wait_ge(s_rank, 1)
            cv = cmp.rearrange("p (e h) -> p e h", h=NTHR + 1)
            link(nc.vector.tensor_tensor(cv, ps[0][:, NT * NE:(NT + 1) * NE].unsqueeze(2).to_broadcast([P, NE, NTHR + 1]),
                                         thr.unsqueeze(1).to_broadcast([P, NE, NTHR + 1]), ALU.is_gt))
            link(nc.vector.tensor_reduce(pfx[0][:, 16:16 + NE], cv, AX.X, ALU.add))
            nc.vector.tensor_scalar(nbn, pfx[0][:, 16:16 + NE], -1.0, None, ALU.mult)
            for i, sh in enumerate((1, 2, 4, 8, 16)):
                src, dst = pfx[i % 2], pfx[(i + 1) % 2]
                link(nc.vector.tensor_tensor(dst[:, 16:16 + NE], src[:, 16:16 + NE], src[:, 16 - sh:16 - sh + NE], ALU.add))
            last = pfx[1][:, 16:16 + NE]
            nc.vector.tensor_copy(bound[0:1, 1:NE + 1], last[0:1, :])
            nc.vector.tensor_copy(rti[0:1, 15:16], last[0:1, NE - 1:NE])
            link(nc.vector.tensor_tensor(sbase, last, nbn, ALU.add))
            link(nc.vector.scalar_tensor_tensor(out=p32.rearrange("p (t e) -> p t e", t=NT),
                                                in0=sbase.unsqueeze(1).to_broadcast([P, NT, NE]), scalar=float(T),
                                                in1=ps[0][:, 0:NT * NE].rearrange("p (t e) -> p t e", t=NT),
                                                op0=ALU.mult, op1=ALU.add))
            for k in range(2):
                oh = ohe[:, k * NT * NE:(k + 1) * NT * NE]
                link(nc.vector.tensor_tensor(oh, oh, p32, ALU.mult))
            link(nc.vector.tensor_reduce(slf, ohe.rearrange("p (i e) -> p i e", e=NE), AX.X, ALU.add))
            link(nc.vector.tensor_copy(rti[:, 0:2 * NT], slf))
            nc.vector.tensor_scalar(bound[0:1, PAIRS:PAIRS + 1], rti[0:1, 15:16], 1, None, ALU.arith_shift_right)
            nc.vector.tensor_scalar(rti[0:1, 31:32], rti[0:1, 15:16], 1, None, ALU.arith_shift_right)
            nc.vector.tensor_scalar(bound[0:1, ODD:ODD + 1], rti[0:1, 15:16], 1, None, ALU.bitwise_and)
            nc.vector.tensor_scalar(rti[:, 16:16 + 2 * NT], rti[:, 0:2 * NT], T.bit_length() - 1, None, ALU.arith_shift_right)
            link(nc.vector.tensor_scalar(rti[:, 32:32 + 2 * NT], rti[:, 0:2 * NT], T - 1, None, ALU.bitwise_and))
            nc.vector.tensor_scalar(bound[0:1, LASTP:LASTP + 1], rti[0:1, 31:32], -1, None, ALU.add)
            link(nc.vector.tensor_tensor(ohq, iotaq.unsqueeze(1).to_broadcast([P, 2 * NT, NBLK]),
                                         rti[:, 16:16 + 2 * NT].unsqueeze(2).to_broadcast([P, 2 * NT, NBLK]), ALU.is_equal))
            nc.vector.tensor_tensor(ohr, iotar.unsqueeze(1).to_broadcast([P, 2 * NT, T]),
                                    rti[:, 32:32 + 2 * NT].unsqueeze(2).to_broadcast([P, 2 * NT, T]), ALU.is_equal)
            nc.vector.tensor_tensor(ohq, ohq, rowv.unsqueeze(2).to_broadcast([P, 2 * NT, NBLK]), ALU.mult).then_inc(s_ab, 1)
            dve.wait_ge(s_inv, 1)
            link(nc.vector.tensor_scalar(vrow, ps[2][:, 0:NBLK], -1.0, float(PAD), ALU.mult, ALU.add))
            nc.vector.tensor_scalar(sidx[:, 0:NBLK], vrow, 2.0, halfp, ALU.mult, ALU.add)
            link(nc.vector.tensor_scalar(vge, vrow, float(NTOK), -float(NTOK), ALU.is_ge, ALU.mult))
            link(nc.vector.tensor_tensor(gidx[:, 0:NBLK], vrow[0:T, :], vge[0:T, :], ALU.add))
            nc.vector.memset(mark[:, 0:1], 1.0).then_inc(s_yc, 1)
            nc.vector.memset(mark[:, 1:2], 1.0).then_inc(s_tab, 1)
            dve.wait_ge(s_ex, 2)
            link(nc.vector.tensor_reduce(pgr, e4.rearrange("p (t g) -> p t g", g=NG), AX.X, ALU.add))
            link(nc.vector.tensor_scalar(ngm, dlt, 1.0, None, ALU.add))
            link(nc.vector.tensor_tensor(pgr, pgr, ngm, ALU.mult))
            link(nc.vector.reciprocal(w12[:, 0:NT], pgr))
            link(nc.vector.tensor_tensor(w12[:, NT:2 * NT], w12[:, 0:NT], dlt, ALU.mult))

            dve.wait_ge(s_tab, 1)
            pairs = dve.value_load(bound[0:1, PAIRS:PAIRS + 1], min_val=NE // 2, max_val=NBLK // 2)
            odd = dve.value_load(bound[0:1, ODD:ODD + 1], min_val=0, max_val=1)

            def move(q, b):
                dve.wait_ge(s_gath[b], q * 16 + 16)
                if not isinstance(q, int) or b:
                    dve.wait_ge(s_xt_ps, q * 2 + b)
                nc.vector.tensor_copy(xrow, stage[b]).then_inc(s_mv, 1)

            def block_of(q, b):
                dve.wait_ge(s_silu, q * 2 + (b + 1))
                nc.vector.tensor_tensor(hid, sg_m, ps[1][:, P:2 * P], ALU.mult).then_inc(s_hid, 1)
                move(q + 1, b)
                dve.wait_ge(s_hT_ps, q * 2 + (b + 1))
                nc.vector.tensor_copy(hidT, ps[2][:, 0:P]).then_inc(s_hidT, 1)

            dve.wait_ge(s_hout, 16 * 5)
            move(0, 0)
            move(0, 1)
            with nc.vector.Fori(0, pairs) as q:
                for b in range(2):
                    block_of(q, b)
            with nc.vector.If(odd > 0):
                block_of(pairs, 0)

            dve.wait_ge(s_gfin, 16)
            for t in range(NT):
                n = TROWS[t]
                xt = x1[0:n, t, :]
                dve.wait_ge(s_yg[t], 32)
                for k in range(2):
                    link(nc.vector.scalar_tensor_tensor(out=xt, in0=yg[k][t][0:n, :], scalar=w12[0:n, k * NT + t:k * NT + t + 1],
                                                        in1=xt, op0=ALU.mult, op1=ALU.add))
                nc.vector.memset(mark, 1.0).then_inc(s_fin, 1)
                dve.wait_ge(s_rms3, t + 1)
                rstd(16, n, t)
                nc.vector.scalar_tensor_tensor(out=xt, in0=xt, scalar=small[0:n, 40 + t:41 + t], in1=gfin[0:n, :],
                                               op0=ALU.mult, op1=ALU.mult).then_inc(s_fin, 1)

        @block.tensor
        def _(pe):
            mm = nc.tensor.matmul
            tr = nc.tensor.transpose
            pe.wait_ge(s_const, NCON)
            pe.wait_ge(s_gmix, 16)
            tr(ps[7][:, 0:KC], grow[:, :], ident[0:KC, 0:KC]).then_inc(s_gT, 1)

            def params():
                pe.wait_ge(s_par, 16 * 8)
                for c in range(CC):
                    cs = slice(c * P, (c + 1) * P)
                    tr(ps[6][:, c * NP:(c + 1) * NP], prow[:, cs], ident[0:NP, 0:NP])
                    tr(ps[6][:, 256 + c * NS * HA:256 + (c + 1) * NS * HA], sa_rows[:, cs], ident[0:NS * HA, 0:NS * HA])
                    for i in range(2):
                        at = (c % 2) * NS * HB + i * QR
                        ins = tr(ps[4 + c // 2][:, at:at + QR], sb_rows[0:QR, i * DA + c * P:i * DA + (c + 1) * P], ident[0:QR, 0:QR])
                ins.then_inc(s_pT, 1)

            for t in range(NT):
                n = TROWS[t]
                pe.wait_ge(s_xn, t + 1)
                if t >= 2:
                    pe.wait_ge(s_hT, t - 1)
                for k in range(KC):
                    ins = tr(ps[2 * (t % 2) + k // 4][:, (k % 4) * n:(k % 4 + 1) * n], xn[0:n, t % 2, k * P:(k + 1) * P],
                             ident[0:n, 0:n])
                ins.then_inc(s_xT, 1)
                if t == NT - 2:
                    params()

            def chunk(name, c, bank):
                for k in range(KC):
                    for j in range(2):
                        ins = mm(ps[2 * bank + j][:, 0:HALF], sec[name][:, k, c * P:(c + 1) * P],
                                 hT[:, k, j * HALF:(j + 1) * HALF], start=(k == 0), stop=(k == KC - 1))
                ins.then_inc(s_chunk, 1)

            pe.wait_ge(s_hT, NT)
            for c in range(CC):
                for i, name in enumerate(("vb", "gb")):
                    if c == 0:
                        pe.wait_ge(s_w[name], 16)
                    else:
                        pe.wait_ge(s_evac, 2 * c + i - 1)
                    chunk(name, c, i)

            def rows_out(bank, n, src):
                for c in range(CC):
                    ins = tr(ps[bank][0:n, c * P:(c + 1) * P], src(c), ident[:, :])
                ins.then_inc(s_hist, 1)

            for c in range(CC):
                for i, name in enumerate(("c", "va", "b")):
                    if c == 0:
                        pe.wait_ge(s_w[name], 16)
                        if i < 2:
                            pe.wait_ge(s_evac, 2 * CC - 1 + i)
                        else:
                            pe.wait_ge(s_hist, 1)
                    else:
                        pe.wait_ge(s_evac, 2 * CC + 3 * (c - 1) + i + 1)
                    chunk(name, c, i)
                    if (c, i) == (2, 0):
                        pe.wait_ge(s_packb, CC)
                        rows_out(6, HB, lambda c: ub[:, c, SEQ:SEQ + HB])
                        rows_out(7, QR, lambda c: hist_b[:, c, 0:QR])
                    if (c, i) == (2, 2):
                        pe.wait_ge(s_histc, 1)
                        rows_out(6, QR, lambda c: hist_b[:, c, QR:2 * QR])
                    if (c, i) == (3, 0):
                        pe.wait_ge(s_histc, 2)
                        pe.wait_ge(s_cb, 1)
                        for j in range(2):
                            for k in range(CC):
                                ins = mm(ps[6 + j][:, 0:HALF], lnmean[:, :], z[:, CC + k, j * HALF:(j + 1) * HALF],
                                         start=(k == 0), stop=(k == CC - 1))
                        ins.then_inc(s_mu, 1)
                    if (c, i) == (3, 1):
                        pe.wait_ge(s_sqb, CC)
                        for j in range(2):
                            for k in range(CC):
                                ins = mm(ps[6 + j][:, 0:HALF], lnmean[:, :], sq[:, k, j * HALF:(j + 1) * HALF],
                                         start=(k == 0), stop=(k == CC - 1))
                        ins.then_inc(s_var, 1)
            def output(t, j):
                n = TROWS[t]
                order = list(range(CC, KC)) + list(range(CC))
                for k in order:
                    if (t, j) == (0, 0) and k >= CC:
                        pe.wait_ge(s_zb, k - CC + 1)
                    if (t, j, k) == (0, 0, 0):
                        pe.wait_ge(s_za, CC)
                    ins = mm(ps[2 * (t % 2) + j][0:n, :], z[:, k, t * P:t * P + n], w_out_sb[:, k, j * 512:(j + 1) * 512],
                             start=(k == order[0]), stop=(k == order[-1]))
                return ins

            def h2_transpose(t):
                n = TROWS[t]
                pe.wait_ge(s_h2, t + 1)
                if t == 0:
                    pe.wait_ge(s_evac, 5 * CC)
                else:
                    pe.wait_ge(s_h2T, t)
                for k in range(KC):
                    ins = tr(ps[4 + k // 4][:, (k % 4) * n:(k % 4 + 1) * n], h2[0:n, t % 2, k * P:(k + 1) * P], ident[0:n, 0:n])
                ins.then_inc(s_h2t, 1)

            def logits(t):
                n = TROWS[t]
                pe.wait_ge(s_h2T, t + 1)
                if t >= 2:
                    pe.wait_ge(s_lgc, t - 1)
                else:
                    pe.wait_ge(s_histc, 4)
                for k in range(KC):
                    ins = mm(ps[6 + t % 2][0:n, 0:NG + NE], h2T[:, t % 2, k, 0:n], wrv[:, k, :], start=(k == 0), stop=(k == KC - 1))
                ins.then_inc(s_lg, 1)

            pe.wait_ge(s_wout, 16)
            pe.wait_ge(s_evac, 5 * CC - 1)
            pe.wait_ge(s_rp, 16 * (NG + 3))
            for t in range(NT):
                if t >= 2:
                    pe.wait_ge(s_x1, t - 1)
                if TROWS[t] > T:
                    output(t, 0)
                    if t:
                        h2_transpose(t - 1)
                    output(t, 1).then_inc(s_o, 1)
                else:
                    h2_transpose(t - 1)
                    for k in range(KC):
                        for j in range(2):
                            ins = mm(ps[2 * (t % 2) + j][j * T:j * T + TROWS[t], :], z[:, k, t * P:NTOK],
                                     w_out_sb[:, k, j * 512:(j + 1) * 512], start=(k == 0), stop=(k == KC - 1))
                    ins.then_inc(s_o, 1)
                if t == 0:
                    pe.wait_ge(s_packa, CC)
                    rows_out(6, HA, lambda c: ua[:, c, SEQ:SEQ + HA])
                    rows_out(7, NS * HA, lambda c: hist_a[:, c, :])
                else:
                    logits(t - 1)
            h2_transpose(NT - 1)
            logits(NT - 1)

            pe.wait_ge(s_x1, NT)
            pe.wait_ge(s_mask, 1)
            for t in range(NT + 1):
                for u in range(min(t + 1, NT)):
                    n = TROWS[u]
                    ins = mm(ps[0][:, t * NE:(t + 1) * NE], (before if u == t else onesb)[0:n, :],
                             maskb[0:n, u * NE:(u + 1) * NE], start=(u == 0), stop=(u == min(t, NT - 1)))
            ins.then_inc(s_rank, 1)
            pe.wait_ge(s_ab, 1)
            for i in range(2 * NT):
                n = TROWS[i % NT]
                for h in range(2):
                    ins = mm(ps[2][h * T:(h + 1) * T, 0:NBLK], ohr[0:n, i, :], ohq[0:n, i, :],
                             start=(i == 0), stop=(i == 2 * NT - 1))
            ins.then_inc(s_inv, 1)

            wgu = [w.rearrange("p (w k f) -> p w k f", w=2, k=KC) for w in slot_gu]
            wdn = [w.rearrange("p (c d) -> p c d", c=F // P) for w in slot_dn]

            def tokens():
                for k in range(KC):
                    ins = tr(ps[0][:, k * T:(k + 1) * T], xrow[:, k * P:(k + 1) * P], ident[0:T, 0:T])
                ins.then_inc(s_xt_ps, 1)

            def gate_up(i, g):
                pe.wait_ge(s_xt, g + 1)
                for k in range(KC):
                    for h in range(2):
                        ins = mm(ps[1][h * T:(h + 1) * T, 0:2 * P].rearrange("p (w f) -> p w f", w=2), xT[:, k, :],
                                 wgu[i][:, :, k, h * P:(h + 1) * P], start=(k == 0), stop=(k == KC - 1))
                ins.then_inc(s_gu, 1)
                pe.wait_ge(s_mv, g + 2)
                mm(ps[5][0:32, 0:1], onesb[:, 0:32], onesb[:, 0:1], start=True, stop=True)
                tokens()

            def down(i, n):
                pe.wait_ge(s_hidT, n)
                pe.wait_ge(s_yc, n)
                for c in range(F // P):
                    for h in range(2):
                        ins = mm(ps[3][h * T:(h + 1) * T, :], hidT[:, c * T:(c + 1) * T], wdn[i][:, c, h * 512:(h + 1) * 512],
                                 start=(c == 0), stop=(c == F // P - 1))
                ins.then_inc(s_down, 1)

            def hid_transpose(g):
                pe.wait_ge(s_hid, g + 1)
                tr(ps[2][:, 0:P], hid, ident[:, :]).then_inc(s_hT_ps, 1)

            pe.wait_ge(s_tab, 1)
            pe.wait_ge(s_mv, 1)
            tokens()
            def expert(it, i):
                first = pe.value_load(bound[0:1, bass.ds(it * NSLOT + i, 1)], min_val=0, max_val=NBLK - 1)
                end = pe.value_load(bound[0:1, bass.ds(it * NSLOT + i + 1, 1)], min_val=1, max_val=NBLK)
                pe.wait_ge(s_wexp[i][0], it * 16 + 16)
                pe.wait_ge(s_wexp[i][1], it * 16 + 16)
                gate_up(i, first)
                if i:
                    down(i - 1, first)
                elif isinstance(it, int):
                    down(NSLOT - 1, first)
                else:
                    with pe.If(it > 0):
                        down(NSLOT - 1, first)
                pe.wait_ge(s_wexp[i][2], it * 16 + 16)
                hid_transpose(first)
                with pe.If(end > first + 1):
                    with pe.Fori(first + 1, end) as g:
                        gate_up(i, g)
                        down(i, g)
                        hid_transpose(g)

            with pe.Fori(0, NE // NSLOT) as it:
                for i in range(NSLOT):
                    expert(it, i)
            for i in range(NE % NSLOT):
                expert(NE // NSLOT, i)
            nblk = pe.value_load(bound[0:1, NE:NE + 1], min_val=NE, max_val=NBLK)
            down((NE - 1) % NSLOT, nblk)


_INS = ["x_prompt", "x_sample", "state_conv_a", "state_conv_b", "g_mix", "w_in", "conv_a_w", "conv_b_w",
        "conv_b_bias", "ln_g", "ln_b", "w_out", "g_ffn", "w_coarse", "b_coarse", "w_fine", "b_fine",
        "w_gate", "w_up", "w_down", "g_final"]
_OUTS = [(1, SEQ, D), (NS, SL, D), (1, 1, HA, DA), (1, 1, HB, DA), (1, NS, HA, DA), (1, NS, HB, DA)]


def kernel(**inputs):
    import numpy as _np
    import concourse.bacc as _bacc
    from concourse import mybir as _mybir
    from concourse.bass_utils import run_bass_kernel_spmd as _run

    nc = _bacc.Bacc("TRN2", target_bir_lowering=False, num_devices=1)
    arrays, args, outs = {}, {}, []
    for name in _INS:
        v = _np.ascontiguousarray(inputs[name])
        arrays[f"in_{name}"] = v
        args[name] = nc.dram_tensor(f"in_{name}", v.shape, _mybir.dt.from_np(v.dtype), kind="ExternalInput").ap()
    for i, shape in enumerate(_OUTS):
        outs.append(nc.dram_tensor(f"out_{i}", shape, _mybir.dt.float32, kind="ExternalOutput").ap())
    build_step(nc, args, outs)
    r = _run(nc, [arrays], core_ids=[0])
    return tuple(r.results[0][f"out_{i}"] for i in range(len(_OUTS)))
```

```python
import concourse.bass as bass
from concourse import mybir
from contextlib import ExitStack

D = 1024
P = 128
KC = D // P
SEQ = 512
NS, SL = 8, 8
NTOK = SEQ + NS * SL
NT = (NTOK + P - 1) // P
TROWS = [min(P, NTOK - t * P) for t in range(NT)]
HALF = NTOK // 2
DA = 512
CC = DA // P
KA, KB = 3, 31
HA, HB = KA - 1, KB - 1
UA = HA + SEQ + NS * (HA + SL)
UB = HB + SEQ + NS * (HB + SL)
SA, SB = HA + SEQ, HB + SEQ
WA, WB = HA + SL, HB + SL
NG, EG = 4, 8
NE = NG * EG
F = 256
T = 64
NSLOT = 6
NBLK = NE + (2 * NTOK - 1) // T
NIDX = NBLK + 4
PAD = 2048
QR = NS * HB // 2
XN_DVE = 3
RMS_EPS, LN_EPS = 1e-6, 1e-5


def build_step(nc, a, out):
    fp32, bf16 = mybir.dt.float32, mybir.dt.bfloat16
    i32, u32 = mybir.dt.int32, mybir.dt.uint32
    ALU = mybir.AluOpType
    ACT = mybir.ActivationFunctionType
    AX = mybir.AxisListType
    y_prompt, y_sample, na_p, nb_p, na_s, nb_s = out

    ctx = ExitStack()
    with ctx:
        def sb(name, shape, dt=fp32):
            return ctx.enter_context(nc.sbuf_tensor(name, shape, dt))

        def sem(name):
            return ctx.enter_context(nc.semaphore(name))

        h2_dram = nc.dram_tensor("h2_rows", (NTOK, D), fp32, kind="Internal").ap()
        y_dram = nc.dram_tensor("y_rows", (2 * NTOK, D), fp32, kind="Internal").ap()
        y_half = y_dram.rearrange("r (h d) -> (r h) d", h=2)

        PART = KC * F
        RX = sb("region_x", [P, NT * D])
        RH = sb("region_h", [P, NT * D])
        RW = sb("region_w", [P, 5 * KC * DA])
        SLOT0 = sb("slot0", [P, 3 * PART])
        ub_t = sb("ub", [P, CC * UB])
        ua_t = sb("ua", [P, CC * UA])
        z_t = sb("z", [P, KC * NTOK])

        x_in = RX[:, :].rearrange("p (t d) -> p t d", t=NT)
        hT = RH[:, 0:KC * NTOK].rearrange("p (k n) -> p k n", k=KC)
        x1 = RH[:, :].rearrange("p (t d) -> p t d", t=NT)
        SEC = KC * DA
        sec = {n: RW[:, i * SEC:(i + 1) * SEC].rearrange("p (k n) -> p k n", k=KC)
               for i, n in enumerate(["vb", "gb", "c", "va", "b"])}
        w_out_sb = RW[:, 0:2 * SEC].rearrange("p (k n) -> p k n", k=KC)
        places = [(SLOT0, 0, SLOT0, 2 * PART),
                  (RW, 2 * SEC, RW, 2 * SEC + 2 * PART),
                  (RW, 2 * SEC + 3 * PART, RW, 2 * SEC + 5 * PART),
                  (RW, 0, RW, 2 * PART),
                  (z_t, 0, RW, 3 * PART),
                  (RX, D, ub_t, D)]
        slot_gu = [reg[:, lo:lo + 2 * PART] for reg, lo, _, _ in places]
        slot_dn = [reg[:, lo:lo + PART] for _, _, reg, lo in places]
        ub = ub_t[:, :].rearrange("p (c n) -> p c n", c=CC)
        ua = ua_t[:, :].rearrange("p (c n) -> p c n", c=CC)
        z = z_t[:, :].rearrange("p (c n) -> p c n", c=KC)
        xn = z_t[:, 0:2 * D].rearrange("p (b d) -> p b d", b=2)
        sqj = z_t[:, 2 * D:3 * D]
        st = [RX[:, i * NTOK:(i + 1) * NTOK] for i in range(5)]
        tA = RX[:, 5 * NTOK:5 * NTOK + UA]
        tB = RX[:, 5 * NTOK + UA:5 * NTOK + 2 * UA]
        rs = RX[:, 5 * NTOK + 2 * UA:6 * NTOK + 2 * UA]
        sq = ub_t[:, 0:CC * NTOK].rearrange("p (c n) -> p c n", c=CC)
        h2T = RX[:, 0:D].rearrange("p (k n) -> p k n", k=KC)
        h2 = RX[:, D:3 * D].rearrange("p (b d) -> p b d", b=2)
        gffn = ub_t[:, 0:D]
        gfin = ub_t[:, 0:D]
        stage = [RX[0:T, 0:D], RX[T:P, 0:D]]
        xT = z_t[:, 2 * PART:2 * PART + KC * T].rearrange("p (k n) -> p k n", k=KC)
        yblk = [ua_t[:, 3 * P + b * D // 2:3 * P + (b + 1) * D // 2] for b in range(2)]
        sg_m = ua_t[:, 0:P]
        hid = ua_t[:, P:2 * P]
        hidT = ua_t[:, 2 * P:3 * P]
        yg = [[(SLOT0 if k == 0 else RW)[:, t * D:(t + 1) * D] for t in range(NT)] for k in range(2)]

        ident = sb("ident", [P, P])
        lnmean = sb("lnmean", [P, P])
        before = sb("before", [P, P], bf16)
        onesb = sb("onesb", [P, P], bf16)
        pst = sb("pst", [P, DA])
        prow = pst[0:KB + KA + 3, :]
        grow = sb("grow", [KC, P])
        par = sb("par", [P, CC * (KB + KA + 3)])
        gmix = sb("gmix", [P, KC])
        sa_rows = sb("sa_rows", [NS * HA, DA])
        sb_rows = sb("sb_rows", [P, 2 * DA])
        st_b = sb_rows
        xrow = sb_rows[0:T, :]
        st_p = pst
        hist_b = sb("hist_b", [P, CC * NS * HB])[:, :].rearrange("p (c n) -> p c n", c=CC)
        hist_a = sb("hist_a", [P, CC * NS * HA])[:, :].rearrange("p (c n) -> p c n", c=CC)
        wr = sb("wr", [P, KC * (NG + NE)])
        rbias = sb("rbias", [P, NG + NE])
        small = sb("small", [P, 64])
        lg = sb("lg", [P, NT * (NG + NE)])
        RTW = 900
        rt = sb("rt", [P, RTW])
        rti = sb("rti", [P, 160], i32)
        rtu = sb("rtu", [P, 32 + 8 * NT], u32)
        maskb = sb("maskb", [P, NT * NE], bf16)
        gidx = sb("gidx", [T, NIDX], u32)
        sidx = sb("sidx", [P, NIDX], u32)
        gcol = sb("gcol", [T, 2], u32)
        scol = sb("scol", [P, 2], u32)
        big = sb("big", [1, NIDX], i32)
        bound = sb("bound", [1, NE + 4], i32)
        PAIRS, ODD, LASTP = NE + 1, NE + 2, NE + 3

        eps_rms, eps_ln = small[:, 60:61], small[:, 61:62]
        carry = sb("carry", [P, 4])[:, :]
        NCON = 22 + 2 * CC
        NP = KB + KA + 3
        parv = par[:, :].rearrange("p (c n) -> p c n", c=CC)

        def wB(c, j):
            return parv[:, c, j:j + 1]

        def wA(c, j):
            return parv[:, c, KB + j:KB + j + 1]

        ps = [ctx.enter_context(nc.psum_tensor(f"bank{i}", [P, 512], fp32)) for i in range(8)]

        s_x = [sem(f"s_xin{t}") for t in range(NT)]
        s_gmix = sem("s_gmix")
        s_par = sem("s_par")
        s_rp = sem("s_rp")
        s_w = {n: sem(f"s_w_{n}") for n in ["vb", "gb", "c", "va", "b"]}
        s_w0 = {n: sem(f"s_w0_{n}") for n in ["vb", "gb"]}
        s_wout = sem("s_wout")
        s_xr = sem("s_xr")
        s_gf = sem("s_gf")
        s_gfin = sem("s_gfin")
        s_const = sem("s_const")
        s_const0 = sem("s_const0")
        s_sq1 = sem("s_sq1")
        s_rms1, s_rms2, s_rms3, s_lnsd = sem("s_rms1"), sem("s_rms2"), sem("s_rms3"), sem("s_lnsd")
        s_xn = sem("s_xn")
        s_xT = sem("s_xT")
        s_hT = sem("s_hT")
        s_rstd1 = sem("s_rstd1")
        s_gT = sem("s_gT")
        s_pT = sem("s_pT")
        s_chunk = sem("s_chunk")
        s_evac = sem("s_evac")
        s_ub = sem("s_ub")
        s_ua = sem("s_ua")
        s_za = sem("s_za")
        s_pa = sem("s_pa")
        s_conv = sem("s_conv")
        s_cb = sem("s_cb")
        s_mu = sem("s_mu")
        s_dev = sem("s_dev")
        s_sqb = sem("s_sqb")
        s_sqs = sem("s_sqs")
        s_var = sem("s_var")
        s_zn = sem("s_zn")
        s_zb = sem("s_zb")
        s_hist = sem("s_hist")
        s_histc = sem("s_histc")
        s_packb = sem("s_packb")
        s_packa = sem("s_packa")
        s_hout = sem("s_hout")
        s_o = sem("s_o")
        s_x1 = sem("s_x1")
        s_sq2 = sem("s_sq2")
        s_h2 = sem("s_h2")
        s_h2d = [sem(f"s_h2d{i}") for i in range(2)]
        s_h2t = sem("s_h2t")
        s_h2T = sem("s_h2T")
        s_lg = sem("s_lg")
        s_lgc = sem("s_lgc")
        s_dve = sem("s_dve")
        s_ex = sem("s_ex")
        s_mask = sem("s_mask")
        s_rank = sem("s_rank")
        s_ranked = sem("s_ranked")
        s_place, s_placed = sem("s_place"), sem("s_placed")
        s_ab = sem("s_ab")
        s_inv = sem("s_inv")
        s_tab = sem("s_tab")
        s_gi = sem("s_gi")
        s_si = sem("s_si")
        s_stage = sem("s_stage")
        s_gath = [sem(f"s_gath{b}") for b in range(2)]
        s_xt_ps = sem("s_xt_ps")
        s_xt = sem("s_xt")
        s_gu = sem("s_gu")
        s_silu = sem("s_silu")
        s_hid = sem("s_hid")
        s_hT_ps = sem("s_hT_ps")
        s_hidT = sem("s_hidT")
        s_down = sem("s_down")
        s_yc = sem("s_yc")
        s_ysc = [sem(f"s_ysc{b}") for b in range(2)]
        s_mv = sem("s_mv")
        s_wexp = [[sem(f"s_wexp{i}_{n}") for n in ("gate", "up", "down")] for i in range(NSLOT)]
        s_yg = [[sem(f"s_yg{k}_{t}") for t in range(NT)] for k in range(2)]
        s_sq3 = sem("s_sq3")
        s_fin1, s_fin = sem("s_fin1"), sem("s_fin")
        s_rstd3, s_scaled = sem("s_rstd3"), sem("s_scaled")
        s_norm = [sem(f"s_norm{t}") for t in range(NT)]
        s_out = sem("s_out")

        at = [0]

        def col(n):
            at[0] += n
            return rt[:, at[0] - n:at[0]]

        iota32, iotaq, rplace = col(NE), col(NBLK), col(P + T + 1)
        row_hi, row_lo = col(2 * NT), col(2 * NT)
        halfp = col(1)
        pgr, ngm, w12 = col(NT), col(NT), col(2 * NT)
        sbase = col(NE)
        pfx = [col(16 + NE), col(16 + NE)]
        pick2 = col(2 * NE)
        m8, v8, grpf, g8 = col(8), col(8 * NT), col(NT), col(1)
        eid2 = col(2 * NT).rearrange("p (t k) -> p t k", k=2)
        e4, fsel, oh4, pick, dlt = col(NG * NT), col(EG * NT), col(NG), col(NE), col(NT)
        mark = col(2)
        more = [col(NBLK), col(NBLK)]
        rankf, rplf = col(2 * NT), col(2 * NT)
        blkf = col(2 * NT)
        assert at[0] <= RTW
        ati = [0]

        def coli(n):
            ati[0] += n
            return rti[:, ati[0] - n:ati[0]]

        ranki, rpl, qrel = coli(2 * NT), coli(2 * NT), coli(2 * NT)
        counti, nbi = coli(NE), coli(16 + NE)
        nblki, pairi, parti, rowi = coli(1), coli(1), coli(1), coli(2 * NT)
        PL = P + T + 1
        ohr = ua_t[:, 0:2 * NT * PL].bitcast(bf16).rearrange("p (h i r) -> p h i r", h=2, i=2 * NT)
        ohe = ua_t[:, 2 * NT * PL:2 * NT * PL + 2 * NT * NE].rearrange("p (i e) -> p i e", e=NE)
        ohq = z_t[:, 2 * PART:2 * PART + NT * NBLK].bitcast(bf16).rearrange("p (i q) -> p i q", i=2 * NT)
        vrow, vtok, vge = [z_t[:, 2 * PART + (NT + i) * NBLK:2 * PART + (NT + i + 1) * NBLK] for i in range(3)]

        def two(v, t):
            return v[:, 2 * t:2 * t + 2]

        def ranks(t):
            bank = 6 + min(t, NT - 1) % 2
            return ps[bank][:, 64 + t * NE:64 + (t + 1) * NE]

        def place_rows(engine, t):
            for i in (2 * t, 2 * t + 1):
                for h, part in enumerate((row_hi, row_lo)):
                    ins = engine.tensor_scalar(ohr[:, h, i, :], rplace, rplf[:, i:i + 1], part[:, i:i + 1],
                                               ALU.is_equal, ALU.mult)
            return ins

        lgv = lg[:, :].rearrange("p (t n) -> p t n", t=NT)
        wrv = wr[:, :].rearrange("p (k n) -> p k n", k=KC)

        def sample(ap, start, width, lo, n):
            return ap[:, start:start + NS * width].rearrange("p (s w) -> p s w", s=NS)[:, :, lo:lo + n]

        block = ctx.enter_context(nc.Block())

        @block.sync
        def _(sp):
            xp, xs = a["x_prompt"][0], a["x_sample"].rearrange("s l d -> (s l) d")

            def rows_of(t):
                return xp[t * P:(t + 1) * P, :] if t < NT - 1 else xs[:, :]

            def load_x(t):
                sp.dma_start(x_in[0:TROWS[t], t, :], rows_of(t)).then_inc(s_x[t], 16)

            load_x(0)
            load_x(1)
            sp.dma_start(grow[:, :], a["g_mix"][0].rearrange("(k p) -> k p", p=P)).then_inc(s_gmix, 16)
            r = 0
            for name, n in (("conv_b_w", KB), ("conv_a_w", KA)):
                sp.dma_start(prow[r:r + n, :], a[name][0]).then_inc(s_par, 16)
                r += n
            load_x(2)
            for name in ("conv_b_bias", "ln_g", "ln_b"):
                sp.dma_start(prow[r:r + 1, :], a[name]).then_inc(s_par, 16)
                r += 1
            load_x(3)
            sp.dma_start(sa_rows[:, :], a["state_conv_a"][0].rearrange("s j c -> (s j) c")).then_inc(s_par, 16)
            hb = a["state_conv_b"][0].rearrange("s j c -> (s j) c")
            for i in range(2):
                sp.dma_start(sb_rows[0:QR, i * DA:(i + 1) * DA], hb[i * QR:(i + 1) * QR, :]).then_inc(s_par, 16)
            load_x(4)
            cols = {"b": 0, "c": 1, "va": 2, "vb": 3, "gb": 4}
            w_in = a["w_in"][0].rearrange("(k p) n -> p k n", p=P)
            for lo, hi, done in ((0, P, s_w0), (P, DA, s_w)):
                for n in ("vb", "gb"):
                    sp.dma_start(sec[n][:, :, lo:hi], w_in[:, :, cols[n] * DA + lo:cols[n] * DA + hi]).then_inc(done[n], 16)
            for n in ("c", "va", "b"):
                sp.dma_start(sec[n], w_in[:, :, cols[n] * DA:(cols[n] + 1) * DA]).then_inc(s_w[n], 16)

            parts = ((a["w_gate"][0].rearrange("e (k p) f -> p e k f", p=P), KC),
                     (a["w_up"][0].rearrange("e (k p) f -> p e k f", p=P), KC),
                     (a["w_down"][0].rearrange("e (c p) d -> p e c d", p=P), F // P))

            def load_part(i, part, e):
                src, k = parts[part]
                dst = slot_dn[i] if part == 2 else slot_gu[i][:, part * PART:(part + 1) * PART]
                sp.dma_start(dst.rearrange("p (k f) -> p k f", k=k),
                             src[:, bass.ds(e, 1), :, :].rearrange("p e k f -> p (e k) f")).then_inc(s_wexp[i][part], 16)

            def load_expert(i, e):
                for part in range(3):
                    load_part(i, part, e)

            load_expert(0, 0)
            sp.wait_ge(s_chunk, 2 * CC)
            sp.dma_start(w_out_sb, a["w_out"][0].rearrange("(k p) n -> p k n", p=P)).then_inc(s_wout, 16)
            sp.wait_ge(s_chunk, 5 * CC)
            for t in range(NT):
                sp.dma_start(x1[0:TROWS[t], t, :], rows_of(t)).then_inc(s_xr, 16)
            load_expert(1, 1)
            load_expert(2, 2)
            sp.wait_ge(s_za, CC)
            sp.wait_ge(s_zn, CC)
            load_part(5, 1, 5)
            load_part(5, 2, 5)
            sp.wait_ge(s_o, NT)
            load_expert(3, 3)
            sp.wait_ge(s_h2, NT)
            load_part(4, 0, 4)
            load_part(4, 1, 4)
            load_part(4, 2, 4)
            for i in range(2):
                sp.wait_ge(s_h2d[i], 16 * ((NT + 1 - i) // 2))
            sp.wait_ge(s_h2t, NT)
            sp.wait_ge(s_gath[0], 16)
            load_part(5, 0, 5)
            sp.wait_ge(s_tab, 1)

            def reload(it, i):
                last = sp.value_load(bound[0:1, bass.ds(it * NSLOT + (i + 1 - NSLOT), 1)],
                                     min_val=1, max_val=NBLK)
                before_i, turn = (i - 1, it + 1) if i else (NSLOT - 1, it)
                for part in range(3):
                    if part < 2:
                        sp.wait_ge(s_wexp[before_i][part + 1], turn * 16)
                    else:
                        sp.wait_ge(s_wexp[i][0], it * 16 + 16)
                    if part == 0:
                        sp.wait_ge(s_gu, last)
                    if part == 2:
                        sp.wait_ge(s_down, last)
                    load_part(i, part, it * NSLOT + i)

            with sp.Fori(1, NE // NSLOT) as it:
                for i in range(NSLOT):
                    reload(it, i)
            for i in range(NE % NSLOT):
                reload(NE // NSLOT, i)
            pairs = sp.value_load(bound[0:1, PAIRS:PAIRS + 1], min_val=NE // 2, max_val=NBLK // 2)
            odd = sp.value_load(bound[0:1, ODD:ODD + 1], min_val=0, max_val=1)
            sp.wait_ge(s_ysc[1], pairs * 16)
            sp.wait_ge(s_ysc[0], (pairs + odd) * 16)
            for t in range(NT):
                for k in range(2):
                    sp.dma_start(yg[k][t][0:TROWS[t], :], y_dram[k * NTOK + t * P:k * NTOK + t * P + TROWS[t], :])\
                      .then_inc(s_yg[k][t], 16)
            for t in range(NT):
                dst = y_prompt[0, t * P:(t + 1) * P, :] if t < NT - 1 else y_sample.rearrange("s l d -> (s l) d")
                sp.wait_ge(s_norm[t], 1)
                sp.dma_start(dst, x1[0:TROWS[t], t, :]).then_inc(s_out, 16)
            sp.wait_ge(s_hout, 16 * 5)
            sp.wait_ge(s_out, 16 * NT)

        @block.scalar
        def _(act):
            def rms(at, n, t, squared, done):
                act.wait_ge(squared, t + 1)
                nc.scalar.activation(small[0:n, at + 24 + t:at + 25 + t], small[0:n, at + t:at + t + 1], ACT.Sqrt,
                                     scale=1.0 / D, bias=eps_rms[0:n, :]).then_inc(done, 1)

            act.wait_ge(s_const, NCON)
            for t in range(NT):
                act.wait_ge(s_x[t], 16)
                if t:
                    act.wait_ge(s_sq1, t)
                n = TROWS[t]
                nc.scalar.activation(sqj[0:n, :], x_in[0:n, t, :], ACT.Square,
                                     accum_out=small[0:n, t:t + 1]).then_inc(s_sq1, 1)
                rms(0, n, t, s_sq1, s_rms1)
            for t in range(XN_DVE, NT):
                n = TROWS[t]
                act.wait_ge(s_rstd1, t - XN_DVE + 1)
                act.wait_ge(s_xT, t - 1)
                nc.scalar.activation(xn[0:n, t % 2, :], x_in[0:n, t, :], ACT.Copy, scale=small[0:n, 24 + t:25 + t])\
                  .then_inc(s_xn, 1)

            def evac(i, bank, dst, func):
                act.wait_ge(s_chunk, i + 1)
                for j in range(2):
                    ins = nc.scalar.activation(dst[:, j * HALF:(j + 1) * HALF], ps[2 * bank + j][:, 0:HALF], func)
                ins.then_inc(s_evac, 1)

            act.dma_start(wrv[:, :, 0:NG], a["w_coarse"][0].rearrange("(k p) g -> p k g", p=P)).then_inc(s_rp, 16)
            for g in range(NG):
                act.dma_start(wrv[:, :, NG + g * EG:NG + (g + 1) * EG],
                              a["w_fine"][0, g].rearrange("(k p) e -> p k e", p=P)).then_inc(s_rp, 16)
            act.dma_start(rbias[:, 0:NG], a["b_coarse"].to_broadcast([P, NG])).then_inc(s_rp, 16)
            act.dma_start(rbias[:, NG:NG + NE],
                          a["b_fine"].rearrange("l g e -> l (g e)").to_broadcast([P, NE])).then_inc(s_rp, 16)

            act.wait_ge(s_xn, NT)
            for c in range(CC):
                if c:
                    act.wait_ge(s_ub, c)
                evac(2 * c, 0, st[0], ACT.Copy)
                evac(2 * c + 1, 1, st[1], ACT.Sigmoid)
            for c in range(CC):
                if c:
                    act.wait_ge(s_ua, c)
                evac(2 * CC + 3 * c, 0, st[2], ACT.Copy)
                if c == 3:
                    for k in range(CC):
                        act.wait_ge(s_dev, k + 1)
                        nc.scalar.activation(sq[:, k, :], z[:, CC + k, :], ACT.Square).then_inc(s_sqb, 1)
                evac(2 * CC + 3 * c + 1, 1, st[3], ACT.Copy)
                if c == 2:
                    act.wait_ge(s_hist, 3)
                    nc.scalar.activation(st_p[0:HB, :], ps[6][0:HB, :], ACT.Copy)
                    nc.scalar.activation(st_b[0:QR, 0:DA], ps[7][0:QR, :], ACT.Copy).then_inc(s_histc, 1)
                if c == 3:
                    act.wait_ge(s_var, 1)
                    for j in range(2):
                        ins = nc.scalar.activation(rs[:, j * HALF:(j + 1) * HALF], ps[6 + j][:, 0:HALF], ACT.Sqrt, bias=eps_ln)
                    ins.then_inc(s_lnsd, 1)
                if c == 3:
                    for k in range(CC):
                        act.wait_ge(s_zn, k + 1)
                        nc.scalar.activation(z[:, CC + k, :], z[:, CC + k, :], ACT.Silu,
                                             scale=parv[:, k, KB + KA + 1:KB + KA + 2],
                                             bias=parv[:, k, KB + KA + 2:KB + KA + 3]).then_inc(s_zb, 1)
                if c:
                    act.wait_ge(s_za, c)
                evac(2 * CC + 3 * c + 2, 2, st[4], ACT.Copy)
                if c == 2:
                    act.wait_ge(s_hist, 4)
                    nc.scalar.activation(st_b[0:QR, DA:2 * DA], ps[6][0:QR, :], ACT.Copy).then_inc(s_histc, 1)
            act.wait_ge(s_var, 1)
            act.dma_start(gffn, a["g_ffn"].to_broadcast([P, D])).then_inc(s_gf, 16)

            for t in range(NT):
                n = TROWS[t]
                act.wait_ge(s_x1, t + 1)
                if t >= 2:
                    act.wait_ge(s_h2d[t % 2], 16 * (t // 2))
                    act.wait_ge(s_h2t, t - 1)
                nc.scalar.activation(h2[0:n, t % 2, :], x1[0:n, t, :], ACT.Square,
                                     accum_out=small[0:n, 8 + t:9 + t]).then_inc(s_sq2, 1)
                rms(8, n, t, s_sq2, s_rms2)
                act.wait_ge(s_h2, t + 1)
                act.dma_start(h2_dram[t * P:t * P + n, :], h2[0:n, t % 2, :]).then_inc(s_h2d[t % 2], 16)
                act.wait_ge(s_h2t, t + 1)
                if t:
                    act.wait_ge(s_lg, t)
                for j in range(2):
                    ins = nc.scalar.activation(h2T[:, 4 * j:4 * j + 4, 0:n],
                                               ps[4 + j][:, 0:4 * n].rearrange("p (k n) -> p k n", k=4), ACT.Copy)
                ins.then_inc(s_h2T, 1)

            act.wait_ge(s_histc, 4)
            act.dma_start(gfin, a["g_final"].rearrange("(l d) -> l d", l=1).to_broadcast([P, D])).then_inc(s_gfin, 16)
            act.dma_start(nb_p[0, 0], st_p[0:HB, :]).then_inc(s_hout, 16)
            act.dma_start(na_s[0].rearrange("s j c -> (s j) c"), st_p[32:32 + NS * HA, :]).then_inc(s_hout, 16)
            act.dma_start(na_p[0, 0], st_p[64:64 + HA, :]).then_inc(s_hout, 16)
            nbs = nb_s[0].rearrange("s j c -> (s j) c")
            for i in range(2):
                act.dma_start(nbs[i * QR:(i + 1) * QR, :], st_b[0:QR, i * DA:(i + 1) * DA]).then_inc(s_hout, 16)

            act.wait_ge(s_mask, NT)
            nc.scalar.activation(e4, e4, ACT.Exp).then_inc(s_ex, 1)
            nc.scalar.activation(dlt, dlt, ACT.Exp).then_inc(s_ex, 1)

            act.wait_ge(s_tab, 1)
            pairs = act.value_load(bound[0:1, PAIRS:PAIRS + 1], min_val=NE // 2, max_val=NBLK // 2)
            last_pair = act.value_load(bound[0:1, LASTP:LASTP + 1], min_val=NE // 2 - 1, max_val=NBLK // 2 - 1)
            odd = act.value_load(bound[0:1, ODD:ODD + 1], min_val=0, max_val=1)

            def tokens_out(n):
                act.wait_ge(s_xt_ps, n)
                nc.scalar.activation(xT[:, :, :].rearrange("p k n -> p (k n)"), ps[0][:, :], ACT.Copy).then_inc(s_xt, 1)

            def silu_gate(n):
                act.wait_ge(s_gu, n)
                nc.scalar.activation(sg_m, ps[1][:, 0:P], ACT.Silu).then_inc(s_silu, 1)

            def outputs_out(q, b):
                act.wait_ge(s_down, q * 2 + (b + 1))
                if not isinstance(q, int):
                    act.wait_ge(s_ysc[b], q * 16)
                nc.scalar.activation(yblk[b], ps[3][:, :], ACT.Copy).then_inc(s_yc, 1)

            tokens_out(1)
            for g in range(3):
                silu_gate(g + 1)
                tokens_out(g + 2)
                if g:
                    outputs_out(0, g - 1)
            with act.Fori(1, last_pair) as q:
                for b in range(2):
                    silu_gate(q * 2 + (b + 2))
                    tokens_out(q * 2 + (b + 3))
                    outputs_out(q, b)
            silu_gate(pairs * 2)
            tokens_out(pairs * 2 + 1)
            outputs_out(last_pair, 0)
            with act.If(odd > 0):
                silu_gate(pairs * 2 + 1)
                tokens_out(pairs * 2 + 2)
            outputs_out(last_pair, 1)
            with act.If(odd > 0):
                outputs_out(pairs, 0)

            nc.scalar.activation(small[:, 62:63], eps_rms, ACT.Sqrt)

            for t in range(NT):
                n = TROWS[t]
                act.wait_ge(s_fin, t + 1)
                nc.scalar.activation(yg[0][t][0:n, :], x1[0:n, t, :], ACT.Square,
                                     accum_out=small[0:n, 16 + t:17 + t]).then_inc(s_sq3, 1)
                rms(16, n, t, s_sq3, s_rms3)
                if t < NT - 1:
                    act.wait_ge(s_rstd3, t + 1)
                    nc.scalar.activation(x1[0:n, t, :], x1[0:n, t, :], ACT.Copy,
                                         scale=small[0:n, 40 + t:41 + t]).then_inc(s_scaled, 1)

        @block.gpsimd
        def _(pool):
            pool.memset(ident[:, :], 0.0).then_inc(s_const0, 1)
            pool.memset(before[:, :], 1.0).then_inc(s_const0, 1)
            pool.memset(lnmean[:, :], 1.0 / DA).then_inc(s_const, 1)
            pool.memset(onesb[:, :], 1.0).then_inc(s_const, 1)
            for c in range(CC):
                pool.memset(ub[:, c, 0:HB], 0.0).then_inc(s_const, 1)
                pool.memset(ua[:, c, 0:HA], 0.0).then_inc(s_const, 1)
            pool.memset(lg[:, :], 0.0).then_inc(s_const, 1)
            pool.memset(m8, -3.0e38).then_inc(s_const, 1)
            pool.memset(carry, 0.0).then_inc(s_const, 1)
            pool.memset(nbi[:, 0:16], 0).then_inc(s_const, 1)
            pool.memset(big[:, NBLK:NIDX], 0).then_inc(s_const, 1)
            for v in pfx:
                pool.memset(v[:, 0:16], 0.0).then_inc(s_const, 1)
            pool.memset(bound[0:1, 0:1], 0).then_inc(s_const, 1)
            pool.memset(gidx[:, NBLK:NIDX], PAD).then_inc(s_const, 1)
            pool.memset(eps_rms, RMS_EPS).then_inc(s_const, 1)
            pool.memset(eps_ln, LN_EPS).then_inc(s_const, 1)
            for v, pat, base, mul in ((iota32, [[1, NE]], 0, 0), (iotaq, [[1, NBLK]], 0, 0),
                                      (rplace[:, 0:P], [[T // 2, 2], [0, 2], [1, T // 2]], 0, 0),
                                      (rplace[:, P:P + T], [[1, T]], 0, 0),
                                      (rplace[:, P + T:PL], [[1, 1]], T // 4, 0), (parti, [[1, 1]], 0, 1),
                                      (rowi, [[-P, NT], [-NTOK, 2]], PAD, -1)):
                pool.iota(v, pattern=pat, base=base, channel_multiplier=mul,
                          allow_small_or_imprecise_dtypes=True).then_inc(s_const, 1)
            pool.wait_ge(s_const0, 2)
            pool.affine_select(out=ident[:, :], in_=ident[:, :], compare_op=ALU.not_equal, fill=1.0,
                               base=0, pattern=[[-1, P]], channel_multiplier=1).then_inc(s_const, 1)
            pool.affine_select(out=before[:, :], in_=before[:, :], compare_op=ALU.is_gt, fill=0.0,
                               base=0, pattern=[[1, P]], channel_multiplier=-1).then_inc(s_const, 1)

            pool.wait_ge(s_hist, 1)
            for c in range(CC):
                pool.wait_ge(s_evac, 2 * c + 2)
                sv = st[0]
                sg = st[1]
                pool.tensor_tensor(ub[:, c, HB:HB + SEQ], sv[:, 0:SEQ], sg[:, 0:SEQ], ALU.mult)
                pool.tensor_tensor(sample(ub[:, c, :], SB, WB, HB, SL),
                                   sv[:, SEQ:NTOK].rearrange("p (s l) -> p s l", s=NS),
                                   sg[:, SEQ:NTOK].rearrange("p (s l) -> p s l", s=NS), ALU.mult).then_inc(s_ub, 1)

                pool.wait_ge(s_ub, c + 1)
                pool.tensor_copy(hist_b[:, c, :].rearrange("p (s j) -> p s j", s=NS),
                                 sample(ub[:, c, :], SB, WB, SL, HB)).then_inc(s_packb, 1)

            n3 = UA - HA
            for c in range(CC):
                pool.wait_ge(s_evac, 2 * CC + 3 * c + 2)
                pool.tensor_tensor(ua[:, c, HA:HA + SEQ], st[2][:, 0:SEQ], st[3][:, 0:SEQ], ALU.mult)
                pool.tensor_tensor(sample(ua[:, c, :], SA, WA, HA, SL),
                                   st[2][:, SEQ:NTOK].rearrange("p (s l) -> p s l", s=NS),
                                   st[3][:, SEQ:NTOK].rearrange("p (s l) -> p s l", s=NS), ALU.mult).then_inc(s_ua, 1)
                pool.wait_ge(s_ua, c + 1)
                pool.tensor_copy(hist_a[:, c, :].rearrange("p (s j) -> p s j", s=NS),
                                 sample(ua[:, c, :], SA, WA, SL, HA)).then_inc(s_packa, 1)
                base = 5 * c
                if c:
                    pool.wait_ge(s_za, c)
                pool.tensor_scalar(tA[:, 0:n3], ua[:, c, 0:n3], wA(c, 0), None, ALU.mult).then_inc(s_pa, 1)
                pool.tensor_scalar(tB[:, 0:n3], ua[:, c, 1:1 + n3], wA(c, 1), None, ALU.mult).then_inc(s_pa, 1)
                pool.wait_ge(s_pa, base + 2)
                pool.tensor_tensor(tA[:, 0:n3], tA[:, 0:n3], tB[:, 0:n3], ALU.add).then_inc(s_pa, 1)
                pool.wait_ge(s_pa, base + 3)
                pool.tensor_scalar(tB[:, 0:n3], ua[:, c, 2:2 + n3], wA(c, 2), None, ALU.mult).then_inc(s_pa, 1)
                pool.wait_ge(s_pa, base + 4)
                pool.tensor_tensor(tA[:, 0:n3], tA[:, 0:n3], tB[:, 0:n3], ALU.add).then_inc(s_pa, 1)
                pool.wait_ge(s_pa, base + 5)
                pool.wait_ge(s_evac, 2 * CC + 3 * c + 3)
                pool.tensor_tensor(z[:, c, 0:SEQ], tA[:, 0:SEQ], st[4][:, 0:SEQ], ALU.mult)
                pool.tensor_tensor(z[:, c, SEQ:NTOK].rearrange("p (s l) -> p s l", s=NS),
                                   tA[:, SA:SA + NS * WA].rearrange("p (s w) -> p s w", s=NS)[:, :, 0:SL],
                                   st[4][:, SEQ:NTOK].rearrange("p (s l) -> p s l", s=NS), ALU.mult).then_inc(s_za, 1)

            for t in range(NT - 1):
                pool.wait_ge(s_place, t + 1)
                place_rows(pool, t).then_inc(s_placed, 1)

            pool.wait_ge(s_ab, 1)
            pool.memset(RX[:, 0:D], 0.0).then_inc(s_stage, 1)
            pool.wait_ge(s_tab, 1)
            pool.wait_ge(s_stage, 1)
            for i in range(2):
                pool.wait_ge(s_h2d[i], 16 * ((NT + 1 - i) // 2))

            def fetch(b, rows):
                pool.indirect_dma_start(stage[b][0:rows, :], None, h2_dram[:, :],
                                        bass.IndirectOffsetOnAxis(ap=gcol[0:rows, b:b + 1], axis=0),
                                        bounds_check=NTOK - 1, oob_is_err=False).then_inc(s_gath[b], 16)

            pool.tensor_copy(gcol[:, :], gidx[:, 0:2]).then_inc(s_gi, 2)
            pool.wait_ge(s_gi, 2)
            for b in range(2):
                fetch(b, T)
            pairs = pool.value_load(bound[0:1, PAIRS:PAIRS + 1], min_val=NE // 2, max_val=NBLK // 2)
            odd = pool.value_load(bound[0:1, ODD:ODD + 1], min_val=0, max_val=1)

            def gather(g, b):
                pool.tensor_copy(gcol[:, b:b + 1], gidx[:, bass.ds(g, 1)]).then_inc(s_gi, 1)
                pool.wait_ge(s_gi, g + 1)
                pool.tensor_tensor(carry[:, 0:1], carry[:, 1:2], carry[:, 1:2], ALU.add)
                size = pool.value_load(big[0:1, bass.ds(g, 1)], min_val=0, max_val=2)
                with pool.If(size > 1):
                    fetch(b, T)
                with pool.If(size < 2):
                    with pool.If(size > 0):
                        fetch(b, T // 2)
                    with pool.If(size < 1):
                        fetch(b, T // 4)

            def scatter(g, b):
                pool.wait_ge(s_yc, g + 2)
                pool.tensor_copy(scol[:, b:b + 1], sidx[:, bass.ds(g, 1)]).then_inc(s_si, 1)
                pool.wait_ge(s_si, g + 1)
                pool.tensor_tensor(carry[:, 2:3], carry[:, 1:2], carry[:, 1:2], ALU.add)
                size = pool.value_load(big[0:1, bass.ds(g, 1)], min_val=0, max_val=2)
                for rows, cond in ((P, size > 1), (P // 2, size < 2)):
                    with pool.If(cond):
                        pool.indirect_dma_start(y_half, bass.IndirectOffsetOnAxis(ap=scol[0:rows, b:b + 1], axis=0),
                                                yblk[b][0:rows, :], None,
                                                bounds_check=4 * NTOK - 1, oob_is_err=False).then_inc(s_ysc[b], 16)

            for g in range(2, 4):
                pool.wait_ge(s_mv, g - 1)
                gather(g, g % 2)
            with pool.Fori(0, pairs) as h:
                for b in range(2):
                    pool.wait_ge(s_mv, h * 2 + (b + 3))
                    gather(h * 2 + (b + 4), b)
                    scatter(h * 2 + b, b)
            with pool.If(odd > 0):
                scatter(pairs * 2, 0)

            for t in range(NT - 1):
                pool.wait_ge(s_scaled, t + 1)
                pool.tensor_tensor(x1[:, t, :], x1[:, t, :], gfin, ALU.mult).then_inc(s_norm[t], 1)

        @block.vector
        def _(dve):
            done = [0]

            def link(ins):
                done[0] += 1
                ins.then_inc(s_dve, 1)
                dve.wait_ge(s_dve, done[0])

            dve.wait_ge(s_const, NCON)
            nc.vector.tensor_scalar(ranki, rowi, 0xFF0, None, ALU.bitwise_and)
            nc.vector.tensor_scalar(rpl, rowi, 0xF, None, ALU.bitwise_and)
            link(nc.vector.tensor_scalar(nblki, parti, 5, 1, ALU.arith_shift_right, ALU.bitwise_and))
            nc.vector.tensor_copy(row_hi, ranki)
            nc.vector.tensor_copy(row_lo, rpl)
            link(nc.vector.tensor_copy(halfp, nblki))

            def rstd(at, n, t):
                c = small[0:n, at + 24 + t:at + 25 + t]
                link(nc.vector.reciprocal(c, c))

            def gain_in(t):
                n = TROWS[t]
                dve.wait_ge(s_xT, t + 1)
                for j in range(2):
                    ins = nc.vector.tensor_tensor(hT[:, 4 * j:4 * j + 4, t * P:t * P + n],
                                                  ps[2 * (t % 2) + j][:, 0:4 * n].rearrange("p (k n) -> p k n", k=4),
                                                  gmix[:, 4 * j:4 * j + 4].unsqueeze(2).to_broadcast([P, 4, n]), ALU.mult)
                ins.then_inc(s_hT, 1)

            def norm_in(t):
                n = TROWS[t]
                dve.wait_ge(s_rms1, t + 1)
                if t >= XN_DVE:
                    c = small[0:n, 24 + t:25 + t]
                    nc.vector.reciprocal(c, c).then_inc(s_rstd1, 1)
                    return
                rstd(0, n, t)
                if t >= 2:
                    dve.wait_ge(s_xT, t - 1)
                nc.vector.tensor_scalar(xn[0:n, t % 2, :], x_in[0:n, t, :], small[0:n, 24 + t:25 + t], None,
                                        ALU.mult).then_inc(s_xn, 1)

            norm_in(0)
            dve.wait_ge(s_gT, 1)
            link(nc.vector.tensor_copy(gmix[:, :], ps[7][:, 0:KC]))
            for t in range(1, NT + 1):
                if t < NT:
                    norm_in(t)
                gain_in(t - 1)
            dve.wait_ge(s_pT, 1)
            link(nc.vector.tensor_copy(par[:, :], ps[6][:, 0:CC * NP]))
            for c in range(CC):
                nc.vector.tensor_copy(sample(ua[:, c, :], SA, WA, 0, HA),
                                      ps[6][:, 256 + c * NS * HA:256 + (c + 1) * NS * HA].rearrange("p (s j) -> p s j", s=NS))
                ins = nc.vector.tensor_copy(sample(ub[:, c, :], SB, WB, 0, HB),
                                            ps[4 + c // 2][:, (c % 2) * NS * HB:(c % 2 + 1) * NS * HB]
                                            .rearrange("p (s j) -> p s j", s=NS))
            ins.then_inc(s_hist, 1)
            dve.wait_ge(s_hist, 1)

            with nc.vector.Fori(0, CC) as c:
                uc = ub[:, bass.ds(c, 1), :].rearrange("p c n -> p (c n)")
                zc = z[:, bass.ds(c + CC, 1), :].rearrange("p c n -> p (c n)")
                pc = parv[:, bass.ds(c, 1), :].rearrange("p c n -> p (c n)")
                dve.wait_ge(s_ub, c + 1)
                zs = zc[:, SEQ:NTOK].rearrange("p (s l) -> p s l", s=NS)
                for j in range(KB):
                    up = uc[:, j:j + SEQ]
                    us = sample(uc, SB, WB, j, SL)
                    if j == 0:
                        b = pc[:, KB + KA:KB + KA + 1]
                        nc.vector.tensor_scalar(zc[:, 0:SEQ], up, pc[:, 0:1], b, ALU.mult, ALU.add).then_inc(s_conv, 1)
                        nc.vector.tensor_scalar(zs, us, pc[:, 0:1], b, ALU.mult, ALU.add).then_inc(s_conv, 1)
                        continue
                    dve.wait_ge(s_conv, c * (2 * KB) + 2 * j - 1)
                    nc.vector.scalar_tensor_tensor(out=zc[:, 0:SEQ], in0=up, scalar=pc[:, j:j + 1], in1=zc[:, 0:SEQ],
                                                   op0=ALU.mult, op1=ALU.add).then_inc(s_conv, 1)
                    dve.wait_ge(s_conv, c * (2 * KB) + 2 * j)
                    nc.vector.scalar_tensor_tensor(out=zs, in0=us, scalar=pc[:, j:j + 1], in1=zs,
                                                   op0=ALU.mult, op1=ALU.add).then_inc(s_conv, 1)
            dve.wait_ge(s_conv, CC * 2 * KB)
            dve.wait_ge(s_hist, 2)

            def add_chunks(v, ready):
                for k in (0, 2):
                    ready(k + 2)
                    ins = nc.vector.tensor_tensor(sq[:, k, :], v(k), v(k + 1), ALU.add)
                link(ins)
                return nc.vector.tensor_tensor(sq[:, 0, :], sq[:, 0, :], sq[:, 2, :], ALU.add)

            add_chunks(lambda k: z[:, CC + k, :], lambda k: None).then_inc(s_cb, 1)
            dve.wait_ge(s_mu, 1)
            for k in range(CC):
                for j in range(2):
                    zz = z[:, CC + k, j * HALF:(j + 1) * HALF]
                    ins = nc.vector.tensor_tensor(zz, zz, ps[6 + j][:, 0:HALF], ALU.subtract)
                ins.then_inc(s_dev, 1)
            add_chunks(lambda k: sq[:, k, :], lambda k: dve.wait_ge(s_sqb, k)).then_inc(s_sqs, 1)
            dve.wait_ge(s_lnsd, 1)
            link(nc.vector.reciprocal(rs, rs))
            for k in range(CC):
                nc.vector.tensor_tensor(z[:, CC + k, :], z[:, CC + k, :], rs, ALU.mult).then_inc(s_zn, 1)
            dve.wait_ge(s_xr, 16 * NT)
            dve.wait_ge(s_rp, 16 * (NG + 3))
            dve.wait_ge(s_gf, 16)

            def logits(t):
                n = TROWS[t]
                dve.wait_ge(s_lg, t + 1)
                nc.vector.tensor_tensor(lgv[0:n, t, :], ps[6 + t % 2][0:n, 0:NG + NE], rbias[0:n, :], ALU.add).then_inc(s_lgc, 1)

            def select(t):
                dve.wait_ge(s_lgc, t + 1)
                link(nc.vector.tensor_copy(m8[:, 0:NG], lgv[:, t, 0:NG]))
                v = v8[:, 8 * t:8 * t + 8]
                vi = rtu[:, 32 + 8 * t:40 + 8 * t]
                link(nc.vector.max(v, m8))
                nc.vector.tensor_scalar(e4[:, NG * t:NG * t + NG], lgv[:, t, 0:NG], v[:, 0:1], None, ALU.subtract)
                link(nc.vector.max_index(vi, v, m8))
                link(nc.vector.tensor_copy(grpf[:, t:t + 1], vi[:, 0:1]))
                nc.vector.tensor_scalar(g8, grpf[:, t:t + 1], float(EG), None, ALU.mult)
                link(nc.vector.tensor_scalar(oh4, iota32[:, 0:NG], grpf[:, t:t + 1], None, ALU.is_equal))
                fs = fsel[:, EG * t:EG * t + EG]
                link(nc.vector.tensor_tensor(pick.rearrange("p (g e) -> p g e", g=NG),
                                             lgv[:, t, NG:NG + NE].rearrange("p (g e) -> p g e", g=NG),
                                             oh4.unsqueeze(2).to_broadcast([P, NG, EG]), ALU.mult))
                link(nc.vector.tensor_reduce(fs, pick.rearrange("p (g e) -> p e g", g=NG), AX.X, ALU.add))
                link(nc.vector.max(v, fs))
                nc.vector.tensor_tensor(dlt[:, t:t + 1], v[:, 1:2], v[:, 0:1], ALU.subtract)
                link(nc.vector.max_index(vi, v, fs))
                link(nc.vector.tensor_scalar(eid2[:, t, :], vi[:, 0:2], g8, None, ALU.add))
                oh = ohe[:, 2 * t:2 * t + 2, :]
                link(nc.vector.tensor_tensor(oh, iota32.unsqueeze(1).to_broadcast([P, 2, NE]),
                                             eid2[:, t, :].unsqueeze(2).to_broadcast([P, 2, NE]), ALU.is_equal))
                nc.vector.tensor_tensor(maskb[:, t * NE:(t + 1) * NE], oh[:, 0, :], oh[:, 1, :], ALU.add).then_inc(s_mask, 1)

            def rank_sum(t):
                return nc.vector.tensor_tensor(pick2.rearrange("p (k e) -> p k e", k=2), ohe[:, 2 * t:2 * t + 2, :],
                                               ranks(t).unsqueeze(1).to_broadcast([P, 2, NE]), ALU.mult)

            def rank_of(t):
                return nc.vector.tensor_reduce(two(rankf, t), pick2.rearrange("p (k e) -> p k e", k=2), AX.X, ALU.add)

            def split(t):
                nc.vector.tensor_scalar(two(qrel, t), two(ranki, t), T.bit_length() - 1, None, ALU.arith_shift_right)
                return nc.vector.tensor_scalar(two(rpl, t), two(ranki, t), T - 1, None, ALU.bitwise_and)

            def place(t):
                dve.wait_ge(s_rank, t + 1)
                rank_sum(t).then_inc(s_ranked, 1)
                dve.wait_ge(s_ranked, t + 1)
                link(rank_of(t))
                link(nc.vector.tensor_copy(two(ranki, t), two(rankf, t)))
                link(split(t))
                nc.vector.tensor_copy(two(rplf, t), two(rpl, t)).then_inc(s_place, 1)

            for t in range(NT):
                n = TROWS[t]
                if t >= 2:
                    place(t - 2)
                dve.wait_ge(s_o, t + 1)
                for j in range(2):
                    xh = x1[0:n, t, j * 512:(j + 1) * 512]
                    lo = 0 if n > T else j * T
                    ins = nc.vector.tensor_tensor(xh, xh, ps[2 * (t % 2) + j][lo:lo + n, :], ALU.add)
                ins.then_inc(s_x1, 1)
                dve.wait_ge(s_rms2, t + 1)
                rstd(8, n, t)
                if t >= 2:
                    dve.wait_ge(s_h2d[t % 2], 16 * (t // 2))
                    dve.wait_ge(s_h2t, t - 1)
                nc.vector.scalar_tensor_tensor(out=h2[0:n, t % 2, :], in0=x1[0:n, t, :], scalar=small[0:n, 32 + t:33 + t],
                                               in1=gffn[0:n, :], op0=ALU.mult, op1=ALU.mult).then_inc(s_h2, 1)
                if t == 0:
                    dve.wait_ge(s_hist, 5)
                    nc.vector.tensor_copy(st_p[64:64 + HA, :], ps[6][0:HA, :]).then_inc(s_histc, 1)
                    dve.wait_ge(s_hist, 6)
                    nc.vector.tensor_copy(st_p[32:32 + NS * HA, :], ps[7][0:NS * HA, :]).then_inc(s_histc, 1)
                else:
                    logits(t - 1)
                    select(t - 1)
            place(NT - 2)
            logits(NT - 1)
            select(NT - 1)

            dve.wait_ge(s_rank, NT)
            nc.vector.tensor_scalar(counti, ranks(NT), 1.0, float(T - 1), ALU.max, ALU.add)
            link(rank_sum(NT - 1))
            nc.vector.tensor_scalar(nbi[:, 16:16 + NE], counti, T.bit_length() - 1, None, ALU.arith_shift_right)
            link(rank_of(NT - 1))
            sums = [nbi, pfx[0], pfx[1], pfx[0], pfx[1], pfx[0]]
            for i, sh in enumerate((1, 2, 4, 8, 16)):
                src, dst = sums[i], sums[i + 1]
                ins = nc.vector.tensor_tensor(dst[:, 16:16 + NE], src[:, 16:16 + NE], src[:, 16 - sh:16 - sh + NE], ALU.add)
                if i == 0:
                    ins = nc.vector.tensor_copy(two(ranki, NT - 1), two(rankf, NT - 1))
                elif i == 1:
                    ins = split(NT - 1)
                elif i == 2:
                    ins = nc.vector.tensor_copy(two(rplf, NT - 1), two(rpl, NT - 1))
                elif i == 3:
                    ins = place_rows(nc.vector, NT - 1)
                link(ins)
            last = sums[-1][:, 16:16 + NE]
            link(nc.vector.tensor_tensor(sbase, last, nbi[:, 16:16 + NE], ALU.subtract))
            link(nc.vector.tensor_tensor(ohe, ohe, sbase.unsqueeze(1).to_broadcast([P, 2 * NT, NE]), ALU.mult))
            nc.vector.tensor_copy(nblki[0:1, :], last[0:1, NE - 1:NE])
            link(nc.vector.tensor_reduce(blkf, ohe, AX.X, ALU.add))
            nc.vector.tensor_copy(bound[0:1, 1:NE + 1], last[0:1, :])
            link(nc.vector.tensor_tensor(blkf, blkf, qrel, ALU.add))
            nc.vector.tensor_tensor(ohq, iotaq.unsqueeze(1).to_broadcast([P, 2 * NT, NBLK]),
                                    blkf.unsqueeze(2).to_broadcast([P, 2 * NT, NBLK]), ALU.is_equal).then_inc(s_ab, 1)
            nc.vector.tensor_scalar(bound[0:1, PAIRS:PAIRS + 1], nblki[0:1, :], 1, None, ALU.arith_shift_right)
            nc.vector.tensor_scalar(bound[0:1, ODD:ODD + 1], nblki[0:1, :], 1, None, ALU.bitwise_and)
            link(nc.vector.tensor_scalar(pairi[0:1, :], nblki[0:1, :], 1, None, ALU.arith_shift_right))
            nc.vector.tensor_scalar(bound[0:1, LASTP:LASTP + 1], pairi[0:1, :], -1, None, ALU.add)
            dve.wait_ge(s_inv, 1)
            nc.vector.tensor_scalar(vtok[0:T + 1, :], ps[1][0:T + 1, 0:NBLK], -1.0, float(PAD), ALU.mult, ALU.add)
            link(nc.vector.tensor_scalar(vrow, ps[0][:, 0:NBLK], -1.0, float(PAD), ALU.mult, ALU.add))
            nc.vector.tensor_scalar(sidx[:, 0:NBLK], vrow, 2.0, halfp, ALU.mult, ALU.add)
            for m, row in zip(more, (T, T // 2)):
                nc.vector.tensor_scalar(m[0:1, :], vtok[row:row + 1, :], float(2 * NTOK), None, ALU.is_lt)
            link(nc.vector.tensor_scalar(vge[0:T, :], vtok[0:T, :], float(NTOK), -float(NTOK), ALU.is_ge, ALU.mult))
            nc.vector.tensor_tensor(big[0:1, 0:NBLK], more[0][0:1, :], more[1][0:1, :], ALU.add)
            link(nc.vector.tensor_tensor(gidx[:, 0:NBLK], vtok[0:T, :], vge[0:T, :], ALU.add))
            nc.vector.memset(mark[:, 0:1], 1.0).then_inc(s_yc, 1)
            nc.vector.memset(mark[:, 1:2], 1.0).then_inc(s_tab, 1)
            dve.wait_ge(s_ex, 2)
            link(nc.vector.tensor_reduce(pgr, e4.rearrange("p (t g) -> p t g", g=NG), AX.X, ALU.add))
            link(nc.vector.tensor_scalar(ngm, dlt, 1.0, None, ALU.add))
            link(nc.vector.tensor_tensor(pgr, pgr, ngm, ALU.mult))
            link(nc.vector.reciprocal(w12[:, 0:NT], pgr))
            link(nc.vector.tensor_tensor(w12[:, NT:2 * NT], w12[:, 0:NT], dlt, ALU.mult))

            dve.wait_ge(s_tab, 1)
            pairs = dve.value_load(bound[0:1, PAIRS:PAIRS + 1], min_val=NE // 2, max_val=NBLK // 2)
            odd = dve.value_load(bound[0:1, ODD:ODD + 1], min_val=0, max_val=1)

            def move(q, b):
                dve.wait_ge(s_gath[b], q * 16 + 16)
                if not isinstance(q, int) or b:
                    dve.wait_ge(s_xt_ps, q * 2 + b)
                nc.vector.tensor_copy(xrow, stage[b]).then_inc(s_mv, 1)

            def block_of(q, b):
                dve.wait_ge(s_silu, q * 2 + (b + 1))
                nc.vector.tensor_tensor(hid, sg_m, ps[1][:, P:2 * P], ALU.mult).then_inc(s_hid, 1)
                move(q + 1, b)
                dve.wait_ge(s_hT_ps, q * 2 + (b + 1))
                nc.vector.tensor_copy(hidT, ps[2][:, 0:P]).then_inc(s_hidT, 1)

            dve.wait_ge(s_hout, 16 * 5)
            move(0, 0)
            move(0, 1)
            with nc.vector.Fori(0, pairs) as q:
                for b in range(2):
                    block_of(q, b)
            with nc.vector.If(odd > 0):
                block_of(pairs, 0)

            dve.wait_ge(s_gfin, 16)
            def rstd_out(t):
                c = small[0:TROWS[t], 40 + t:41 + t]
                dve.wait_ge(s_rms3, t + 1)
                nc.vector.reciprocal(c, c).then_inc(s_rstd3, 1)

            for t in range(NT):
                n = TROWS[t]
                xt = x1[0:n, t, :]
                for k in range(2):
                    dve.wait_ge(s_yg[k][t], 16)
                    ins = nc.vector.scalar_tensor_tensor(out=xt, in0=yg[k][t][0:n, :],
                                                         scalar=w12[0:n, k * NT + t:k * NT + t + 1],
                                                         in1=xt, op0=ALU.mult, op1=ALU.add)
                    if k == 0:
                        ins.then_inc(s_fin1, 1)
                        if t:
                            rstd_out(t - 1)
                        dve.wait_ge(s_fin1, t + 1)
                ins.then_inc(s_fin, 1)
            rstd_out(NT - 1)
            dve.wait_ge(s_rstd3, NT)
            nc.vector.scalar_tensor_tensor(out=xt, in0=xt, scalar=small[0:n, 40 + t:41 + t], in1=gfin[0:n, :],
                                           op0=ALU.mult, op1=ALU.mult).then_inc(s_norm[t], 1)

        @block.tensor
        def _(pe):
            mm = nc.tensor.matmul
            tr = nc.tensor.transpose
            pe.wait_ge(s_const, NCON)
            def keep_busy(n):
                for _ in range(n):
                    mm(ps[5][:, :], onesb[:, :], ident[:, :].bitcast(bf16)[:, 0:2 * P].unsqueeze(1)
                       .to_broadcast([P, 2, 2 * P]), start=True, stop=True)

            keep_busy(12)
            pe.wait_ge(s_gmix, 16)
            tr(ps[7][:, 0:KC], grow[:, :], ident[0:KC, 0:KC]).then_inc(s_gT, 1)

            def params():
                pe.wait_ge(s_par, 16 * 8)
                for c in range(CC):
                    cs = slice(c * P, (c + 1) * P)
                    tr(ps[6][:, c * NP:(c + 1) * NP], prow[:, cs], ident[0:NP, 0:NP])
                    tr(ps[6][:, 256 + c * NS * HA:256 + (c + 1) * NS * HA], sa_rows[:, cs], ident[0:NS * HA, 0:NS * HA])
                    for i in range(2):
                        at = (c % 2) * NS * HB + i * QR
                        ins = tr(ps[4 + c // 2][:, at:at + QR], sb_rows[0:QR, i * DA + c * P:i * DA + (c + 1) * P], ident[0:QR, 0:QR])
                ins.then_inc(s_pT, 1)

            for t in range(NT):
                n = TROWS[t]
                pe.wait_ge(s_xn, t + 1)
                if t >= 2:
                    pe.wait_ge(s_hT, t - 1)
                for k in range(KC):
                    ins = tr(ps[2 * (t % 2) + k // 4][:, (k % 4) * n:(k % 4 + 1) * n], xn[0:n, t % 2, k * P:(k + 1) * P],
                             ident[0:n, 0:n])
                ins.then_inc(s_xT, 1)
                if t == NT - 3:
                    params()

            def chunk(name, c, bank):
                for k in range(KC):
                    for j in range(2):
                        ins = mm(ps[2 * bank + j][:, 0:HALF], sec[name][:, k, c * P:(c + 1) * P],
                                 hT[:, k, j * HALF:(j + 1) * HALF], start=(k == 0), stop=(k == KC - 1))
                ins.then_inc(s_chunk, 1)

            pe.wait_ge(s_hT, NT)
            for c in range(CC):
                for i, name in enumerate(("vb", "gb")):
                    if c == 0:
                        pe.wait_ge(s_w0[name], 16)
                    else:
                        if c == 1:
                            pe.wait_ge(s_w[name], 16)
                        pe.wait_ge(s_evac, 2 * c + i - 1)
                    chunk(name, c, i)

            def rows_out(bank, n, src):
                for c in range(CC):
                    ins = tr(ps[bank][0:n, c * P:(c + 1) * P], src(c), ident[:, :])
                ins.then_inc(s_hist, 1)

            for c in range(CC):
                for i, name in enumerate(("c", "va", "b")):
                    if c == 0:
                        pe.wait_ge(s_w[name], 16)
                        if i < 2:
                            pe.wait_ge(s_evac, 2 * CC - 1 + i)
                        else:
                            pe.wait_ge(s_hist, 1)
                    else:
                        pe.wait_ge(s_evac, 2 * CC + 3 * (c - 1) + i + 1)
                    chunk(name, c, i)
                    if (c, i) == (2, 0):
                        pe.wait_ge(s_packb, CC)
                        rows_out(6, HB, lambda c: ub[:, c, SEQ:SEQ + HB])
                        rows_out(7, QR, lambda c: hist_b[:, c, 0:QR])
                    if (c, i) == (2, 2):
                        pe.wait_ge(s_histc, 1)
                        rows_out(6, QR, lambda c: hist_b[:, c, QR:2 * QR])
                    if (c, i) == (3, 0):
                        pe.wait_ge(s_histc, 2)
                        pe.wait_ge(s_cb, 1)
                        for j in range(2):
                            ins = mm(ps[6 + j][:, 0:HALF], lnmean[:, :], sq[:, 0, j * HALF:(j + 1) * HALF],
                                     start=True, stop=True)
                        ins.then_inc(s_mu, 1)
                    if (c, i) == (3, 1):
                        pe.wait_ge(s_sqs, 1)
                        for j in range(2):
                            ins = mm(ps[6 + j][:, 0:HALF], lnmean[:, :], sq[:, 0, j * HALF:(j + 1) * HALF],
                                     start=True, stop=True)
                        ins.then_inc(s_var, 1)
            def output(t, j):
                n = TROWS[t]
                order = list(range(CC, KC)) + list(range(CC))
                for k in order:
                    if (t, j) == (0, 0) and k >= CC:
                        pe.wait_ge(s_zb, k - CC + 1)
                    if (t, j, k) == (0, 0, 0):
                        pe.wait_ge(s_za, CC)
                    ins = mm(ps[2 * (t % 2) + j][0:n, :], z[:, k, t * P:t * P + n], w_out_sb[:, k, j * 512:(j + 1) * 512],
                             start=(k == order[0]), stop=(k == order[-1]))
                return ins

            def h2_transpose(t):
                n = TROWS[t]
                pe.wait_ge(s_h2, t + 1)
                if t == 0:
                    pe.wait_ge(s_evac, 5 * CC)
                else:
                    pe.wait_ge(s_h2T, t)
                for k in range(KC):
                    ins = tr(ps[4 + k // 4][:, (k % 4) * n:(k % 4 + 1) * n], h2[0:n, t % 2, k * P:(k + 1) * P], ident[0:n, 0:n])
                ins.then_inc(s_h2t, 1)

            def logits(t):
                n = TROWS[t]
                pe.wait_ge(s_h2T, t + 1)
                if t >= 2:
                    pe.wait_ge(s_lgc, t - 1)
                    pe.wait_ge(s_ranked, t - 1)
                else:
                    pe.wait_ge(s_histc, 4)
                for k in range(KC):
                    ins = mm(ps[6 + t % 2][0:n, 0:NG + NE], h2T[:, k, 0:n], wrv[:, k, :], start=(k == 0), stop=(k == KC - 1))
                ins.then_inc(s_lg, 1)

            def rank(t):
                pe.wait_ge(s_mask, t + 1)
                for v in ((t, NT) if t == NT - 1 else (t,)):
                    for u in range(t + 1):
                        n = TROWS[u]
                        ins = mm(ranks(v), (before if u == v else onesb)[0:n, :],
                                 maskb[0:n, u * NE:(u + 1) * NE], start=(u == 0), stop=(u == t))
                ins.then_inc(s_rank, 1)

            pe.wait_ge(s_wout, 16)
            pe.wait_ge(s_evac, 5 * CC - 1)
            pe.wait_ge(s_rp, 16 * (NG + 3))
            for t in range(NT):
                if t >= 2:
                    pe.wait_ge(s_x1, t - 1)
                if TROWS[t] > T:
                    output(t, 0)
                    if t:
                        h2_transpose(t - 1)
                    if t >= 2:
                        rank(t - 2)
                    output(t, 1).then_inc(s_o, 1)
                else:
                    for k in range(KC):
                        if k == KC // 2:
                            h2_transpose(t - 1)
                        if k == KC - 1:
                            rank(t - 2)
                        for j in range(2):
                            ins = mm(ps[2 * (t % 2) + j][j * T:j * T + TROWS[t], :], z[:, k, t * P:NTOK],
                                     w_out_sb[:, k, j * 512:(j + 1) * 512], start=(k == 0), stop=(k == KC - 1))
                    ins.then_inc(s_o, 1)
                if t == 0:
                    pe.wait_ge(s_packa, CC)
                    rows_out(6, HA, lambda c: ua[:, c, SEQ:SEQ + HA])
                    rows_out(7, NS * HA, lambda c: hist_a[:, c, :])
                else:
                    logits(t - 1)
            h2_transpose(NT - 1)
            rank(NT - 2)
            logits(NT - 1)
            rank(NT - 1)

            keep_busy(14)
            pe.wait_ge(s_placed, NT - 1)
            pe.wait_ge(s_ab, 1)
            for i in range(2 * NT):
                n = TROWS[i // 2]
                for h in range(2):
                    start, stop = (i, h) == (0, 0), (i, h) == (2 * NT - 1, 1)
                    mm(ps[0][:, 0:NBLK], ohr[0:n, h, i, 0:P], ohq[0:n, i, :], start=start, stop=stop)
                    ins = mm(ps[1][0:T + 1, 0:NBLK], ohr[0:n, h, i, P:PL], ohq[0:n, i, :], start=start, stop=stop)
            ins.then_inc(s_inv, 1)

            wgu = [w.rearrange("p (w k f) -> p w k f", w=2, k=KC) for w in slot_gu]
            wdn = [w.rearrange("p (c d) -> p c d", c=F // P) for w in slot_dn]

            def tokens():
                for k in range(KC):
                    ins = tr(ps[0][:, k * T:(k + 1) * T], xrow[:, k * P:(k + 1) * P], ident[0:T, 0:T])
                ins.then_inc(s_xt_ps, 1)

            def gate_up(i, g):
                pe.wait_ge(s_xt, g + 1)
                for k in range(KC):
                    for h in range(2):
                        ins = mm(ps[1][h * T:(h + 1) * T, 0:2 * P].rearrange("p (w f) -> p w f", w=2), xT[:, k, :],
                                 wgu[i][:, :, k, h * P:(h + 1) * P], start=(k == 0), stop=(k == KC - 1))
                ins.then_inc(s_gu, 1)
                pe.wait_ge(s_mv, g + 2)
                mm(ps[5][0:32, 0:1], onesb[:, 0:32], onesb[:, 0:1], start=True, stop=True)
                tokens()

            def down(i, n):
                pe.wait_ge(s_hidT, n)
                pe.wait_ge(s_yc, n)
                for c in range(F // P):
                    for quarter in range(4):
                        r0, h = quarter // 2 * (T // 2), quarter % 2
                        ins = mm(ps[3][quarter * 32:(quarter + 1) * 32, :], hidT[:, c * T + r0:c * T + r0 + T // 2],
                                 wdn[i][:, c, h * 512:(h + 1) * 512], start=(c == 0), stop=(c == F // P - 1))
                ins.then_inc(s_down, 1)

            def hid_transpose(g):
                pe.wait_ge(s_hid, g + 1)
                tr(ps[2][:, 0:P], hid, ident[:, :]).then_inc(s_hT_ps, 1)

            keep_busy(31)
            pe.wait_ge(s_tab, 1)
            pe.wait_ge(s_mv, 1)
            tokens()
            def expert(it, i):
                first = pe.value_load(bound[0:1, bass.ds(it * NSLOT + i, 1)], min_val=0, max_val=NBLK - 1)
                end = pe.value_load(bound[0:1, bass.ds(it * NSLOT + i + 1, 1)], min_val=1, max_val=NBLK)
                pe.wait_ge(s_wexp[i][0], it * 16 + 16)
                pe.wait_ge(s_wexp[i][1], it * 16 + 16)
                gate_up(i, first)
                if i:
                    down(i - 1, first)
                elif isinstance(it, int):
                    down(NSLOT - 1, first)
                else:
                    with pe.If(it > 0):
                        down(NSLOT - 1, first)
                pe.wait_ge(s_wexp[i][2], it * 16 + 16)
                hid_transpose(first)
                with pe.If(end > first + 1):
                    with pe.Fori(first + 1, end) as g:
                        gate_up(i, g)
                        down(i, g)
                        hid_transpose(g)

            with pe.Fori(0, NE // NSLOT) as it:
                for i in range(NSLOT):
                    expert(it, i)
            for i in range(NE % NSLOT):
                expert(NE // NSLOT, i)
            nblk = pe.value_load(bound[0:1, NE:NE + 1], min_val=NE, max_val=NBLK)
            down((NE - 1) % NSLOT, nblk)


_INS = ["x_prompt", "x_sample", "state_conv_a", "state_conv_b", "g_mix", "w_in", "conv_a_w", "conv_b_w",
        "conv_b_bias", "ln_g", "ln_b", "w_out", "g_ffn", "w_coarse", "b_coarse", "w_fine", "b_fine",
        "w_gate", "w_up", "w_down", "g_final"]
_OUTS = [(1, SEQ, D), (NS, SL, D), (1, 1, HA, DA), (1, 1, HB, DA), (1, NS, HA, DA), (1, NS, HB, DA)]


def kernel(**inputs):
    import numpy as _np
    import concourse.bacc as _bacc
    from concourse import mybir as _mybir
    from concourse.bass_utils import run_bass_kernel_spmd as _run

    nc = _bacc.Bacc("TRN2", target_bir_lowering=False, num_devices=1)
    arrays, args, outs = {}, {}, []
    for name in _INS:
        v = _np.ascontiguousarray(inputs[name])
        arrays[f"in_{name}"] = v
        args[name] = nc.dram_tensor(f"in_{name}", v.shape, _mybir.dt.from_np(v.dtype), kind="ExternalInput").ap()
    for i, shape in enumerate(_OUTS):
        outs.append(nc.dram_tensor(f"out_{i}", shape, _mybir.dt.float32, kind="ExternalOutput").ap())
    build_step(nc, args, outs)
    r = _run(nc, [arrays], core_ids=[0])
    return tuple(r.results[0][f"out_{i}"] for i in range(len(_OUTS)))
```
